# Optimizing a Trainium2 kernel written in Bass

```python
import math
import jax, jax.numpy as jnp
from jax import lax
import numpy as np

D_MODEL = 1024
BATCH = 1
SEQ = 512
DEPTH = 2

GRID_W = 64
CTX_LEN = 256
N_Q_HEADS = 8
N_KV_HEADS = 2
GQA_GROUP = N_Q_HEADS // N_KV_HEADS
HEAD_DIM = 128
ATTN_WIDTH = N_Q_HEADS * HEAD_DIM
KV_WIDTH = N_KV_HEADS * HEAD_DIM
ROPE_THETA = 10000.0
ROPE_FREQS = HEAD_DIM // 4
Q_BLOCK = 128
ATTN_SCALE = 1.0 / math.sqrt(HEAD_DIM)
GMLP_WIDTH = D_MODEL
GMLP_GROUPS = 4
GMLP_GROUP_DIM = GMLP_WIDTH // GMLP_GROUPS
CHUNK = 128
CONV_WIDTH = D_MODEL
CONV_KERNEL = 31
CONV_PAD = CONV_KERNEL // 2
N_BRANCHES = 3
D_FF = 4 * D_MODEL
EPS = 1e-6
Q_OFF = 0
K_OFF = Q_OFF + ATTN_WIDTH
V_OFF = K_OFF + KV_WIDTH
GU_OFF = V_OFF + KV_WIDTH
GV_OFF = GU_OFF + GMLP_WIDTH
CG_OFF = GV_OFF + GMLP_WIDTH
GATE_OFF = CG_OFF + 2 * CONV_WIDTH
IN_COLS = GATE_OFF + N_BRANCHES * D_MODEL


def rms_norm(x, g):
    xf = x.astype(jnp.float32)
    y = xf * lax.rsqrt(jnp.mean(xf * xf, axis=-1, keepdims=True) + EPS)
    return (y * g.astype(jnp.float32)).astype(x.dtype)

def layer_norm(x, g, b):
    xf = x.astype(jnp.float32)
    mu = jnp.mean(xf, axis=-1, keepdims=True)
    var = jnp.mean(jnp.square(xf - mu), axis=-1, keepdims=True)
    y = (xf - mu) * lax.rsqrt(var + EPS)
    return (y * g.astype(jnp.float32) + b.astype(jnp.float32)).astype(x.dtype)

def modulate(h, shift, scale):
    return h * (1.0 + scale) + shift

def axial_rope_tables(n_rows):
    row = jnp.repeat(jnp.arange(n_rows), GRID_W).astype(jnp.float32)
    col = jnp.tile(jnp.arange(GRID_W), n_rows).astype(jnp.float32)
    inv = ROPE_THETA ** (-jnp.arange(ROPE_FREQS, dtype=jnp.float32) / ROPE_FREQS)
    ang = jnp.concatenate([row[:, None] * inv, col[:, None] * inv], axis=-1)
    return jnp.cos(ang), jnp.sin(ang)

def apply_rope(x, cos, sin):
    half = HEAD_DIM // 2
    x1, x2 = x[..., :half], x[..., half:]
    c = cos[None, :, None, :].astype(x.dtype)
    s = sin[None, :, None, :].astype(x.dtype)
    return jnp.concatenate([x1 * c - x2 * s, x2 * c + x1 * s], axis=-1)

def q_heads(p, q_norm_g):
    B, L, _ = p.shape
    return rms_norm(p[..., Q_OFF:K_OFF].reshape(B, L, N_Q_HEADS, HEAD_DIM), q_norm_g)

def kv_heads(pkv, k_norm_g):
    B, L, _ = pkv.shape
    k = rms_norm(pkv[..., :KV_WIDTH].reshape(B, L, N_KV_HEADS, HEAD_DIM), k_norm_g)
    v = pkv[..., KV_WIDTH:].reshape(B, L, N_KV_HEADS, HEAD_DIM)
    return k, v

def gqa_attend(q, k, v):
    s = jnp.einsum('bqhgd,bkhd->bhgqk', q, k).astype(jnp.float32) * ATTN_SCALE
    p = jax.nn.softmax(s, axis=-1).astype(v.dtype)
    return jnp.einsum('bhgqk,bkhd->bqhgd', p, v)

def latent_attention(q, k_all, v_all):
    B, S = q.shape[0], q.shape[1]
    nb = S // Q_BLOCK
    qb = q.reshape(B, nb, Q_BLOCK, N_KV_HEADS, GQA_GROUP, HEAD_DIM).transpose(1, 0, 2, 3, 4, 5)
    ob = lax.map(lambda qi: gqa_attend(qi, k_all, v_all), qb)
    return ob.transpose(1, 0, 2, 3, 4, 5).reshape(B, S, ATTN_WIDTH)

def chunk_spatial_gate(u, v, ws, bs):
    B, L, _ = v.shape
    nc = L // CHUNK
    vg = v.reshape(B, nc, CHUNK, GMLP_GROUPS, GMLP_GROUP_DIM)
    sv = jnp.einsum('gpq,bnqgc->bnpgc', ws, vg) + bs.T[None, None, :, :, None]
    return u * sv.reshape(B, L, GMLP_WIDTH)

def conformer_conv(a, conv_w, conv_b, norm_g, norm_b, w_o):
    gl = a[..., :CONV_WIDTH] * jax.nn.sigmoid(a[..., CONV_WIDTH:])
    y = lax.conv_general_dilated(gl, conv_w[:, None, :], window_strides=(1,),
                                 padding=[(CONV_PAD, CONV_PAD)],
                                 dimension_numbers=('NWC', 'WIO', 'NWC'),
                                 feature_group_count=CONV_WIDTH) + conv_b
    y = jax.nn.silu(layer_norm(y, norm_g, norm_b))
    return y @ w_o

def mixer_merge(p, attn, w_attn_o, gmlp_norm_g, gmlp_ws, gmlp_bs, w_gmlp_o,
                conv_w, conv_b, conv_norm_g, conv_norm_b, w_conv_o, w_out):
    a_out = attn @ w_attn_o
    gu = jax.nn.gelu(p[..., GU_OFF:GV_OFF])
    gv = rms_norm(jax.nn.gelu(p[..., GV_OFF:CG_OFF]), gmlp_norm_g)
    g_out = chunk_spatial_gate(gu, gv, gmlp_ws, gmlp_bs) @ w_gmlp_o
    c_out = conformer_conv(p[..., CG_OFF:GATE_OFF], conv_w, conv_b, conv_norm_g, conv_norm_b, w_conv_o)
    gates = jax.nn.sigmoid(p[..., GATE_OFF:])
    ga = gates[..., :D_MODEL]
    gg = gates[..., D_MODEL:2 * D_MODEL]
    gc = gates[..., 2 * D_MODEL:]
    return (ga * a_out + gg * g_out + gc * c_out) @ w_out

def sq_relu_mlp(h, w1, w2):
    return jnp.square(jax.nn.relu(h @ w1)) @ w2

def first_inputs(seed: int = 0) -> dict:
    key = jax.random.key(seed)
    ks = jax.random.split(key, 32)
    f32 = jnp.float32

    def nrm(k, shape, scale):
        return jax.random.normal(k, shape, f32) * scale

    def gain(k, shape):
        return 1.0 + 0.1 * jax.random.normal(k, shape, f32)

    L = DEPTH
    return {
        'x': nrm(ks[0], (BATCH, SEQ, D_MODEL), 1.0),
        'c': nrm(ks[1], (BATCH, D_MODEL), 1.0),
        'ctx': nrm(ks[2], (BATCH, CTX_LEN, D_MODEL), 1.0),
        'c_ctx': nrm(ks[3], (D_MODEL,), 1.0),
        'ada_w': nrm(ks[4], (L, D_MODEL, 6 * D_MODEL), 0.5 * D_MODEL ** -0.5),
        'ada_b': nrm(ks[5], (L, 6 * D_MODEL), 0.02),
        'mix_pre_g': gain(ks[6], (L, D_MODEL)),
        'mix_post_g': gain(ks[7], (L, D_MODEL)),
        'w_in': nrm(ks[8], (L, D_MODEL, IN_COLS), D_MODEL ** -0.5),
        'q_norm_g': gain(ks[9], (L, HEAD_DIM)),
        'k_norm_g': gain(ks[10], (L, HEAD_DIM)),
        'w_attn_o': nrm(ks[11], (L, ATTN_WIDTH, D_MODEL), ATTN_WIDTH ** -0.5),
        'gmlp_norm_g': gain(ks[12], (L, GMLP_WIDTH)),
        'gmlp_ws': nrm(ks[13], (L, GMLP_GROUPS, CHUNK, CHUNK), CHUNK ** -0.5),
        'gmlp_bs': gain(ks[14], (L, GMLP_GROUPS, CHUNK)),
        'w_gmlp_o': nrm(ks[15], (L, GMLP_WIDTH, D_MODEL), GMLP_WIDTH ** -0.5),
        'conv_w': nrm(ks[16], (L, CONV_KERNEL, CONV_WIDTH), CONV_KERNEL ** -0.5),
        'conv_b': nrm(ks[17], (L, CONV_WIDTH), 0.02),
        'conv_norm_g': gain(ks[18], (L, CONV_WIDTH)),
        'conv_norm_b': nrm(ks[19], (L, CONV_WIDTH), 0.02),
        'w_conv_o': nrm(ks[20], (L, CONV_WIDTH, D_MODEL), CONV_WIDTH ** -0.5),
        'w_out': nrm(ks[21], (L, D_MODEL, D_MODEL), D_MODEL ** -0.5),
        'ffn_pre_g': gain(ks[22], (L, D_MODEL)),
        'ffn_post_g': gain(ks[23], (L, D_MODEL)),
        'w_ff1': nrm(ks[24], (L, D_MODEL, D_FF), D_MODEL ** -0.5),
        'w_ff2': nrm(ks[25], (L, D_FF, D_MODEL), D_FF ** -0.5),
    }

def first_block(x, c, ctx, c_ctx, ada_w, ada_b, mix_pre_g, mix_post_g, w_in, q_norm_g, k_norm_g,
              w_attn_o, gmlp_norm_g, gmlp_ws, gmlp_bs, w_gmlp_o, conv_w, conv_b, conv_norm_g,
              conv_norm_b, w_conv_o, w_out, ffn_pre_g, ffn_post_g, w_ff1, w_ff2):
    B, S, _ = x.shape
    n_ctx = ctx.shape[1]
    ROWS = S // GRID_W
    cos, sin = axial_rope_tables(ROWS)
    xc = ctx
    for l in range(DEPTH):
        last = l == DEPTH - 1
        mod = (jax.nn.silu(c) @ ada_w[l] + ada_b[l])[:, None, :]
        sh1, sc1, g1, sh2, sc2, g2 = jnp.split(mod, 6, axis=-1)
        modc = jax.nn.silu(c_ctx) @ ada_w[l] + ada_b[l]
        shc1, scc1, gc1, shc2, scc2, gc2 = jnp.split(modc, 6, axis=-1)

        h = modulate(rms_norm(x, mix_pre_g[l]), sh1, sc1)
        hc = modulate(rms_norm(xc, mix_pre_g[l]), shc1, scc1)
        p = h @ w_in[l]
        q = apply_rope(q_heads(p, q_norm_g[l]), cos, sin)
        k, v = kv_heads(p[..., K_OFF:GU_OFF], k_norm_g[l])
        k = apply_rope(k, cos, sin)
        if last:
            kc, vc = kv_heads(hc @ w_in[l][:, K_OFF:GU_OFF], k_norm_g[l])
        else:
            pc = hc @ w_in[l]
            qc = q_heads(pc, q_norm_g[l])
            kc, vc = kv_heads(pc[..., K_OFF:GU_OFF], k_norm_g[l])
        k_all = jnp.concatenate([kc, k], axis=1)
        v_all = jnp.concatenate([vc, v], axis=1)
        attn = latent_attention(q.reshape(B, S, N_KV_HEADS, GQA_GROUP, HEAD_DIM), k_all, v_all)
        y = mixer_merge(p, attn, w_attn_o[l], gmlp_norm_g[l], gmlp_ws[l], gmlp_bs[l], w_gmlp_o[l],
                        conv_w[l], conv_b[l], conv_norm_g[l], conv_norm_b[l], w_conv_o[l], w_out[l])
        x = x + g1 * rms_norm(y, mix_post_g[l])

        h2 = modulate(rms_norm(x, ffn_pre_g[l]), sh2, sc2)
        x = x + g2 * rms_norm(sq_relu_mlp(h2, w_ff1[l], w_ff2[l]), ffn_post_g[l])

        if not last:
            attn_c = gqa_attend(qc.reshape(B, n_ctx, N_KV_HEADS, GQA_GROUP, HEAD_DIM), kc, vc)
            yc = mixer_merge(pc, attn_c.reshape(B, n_ctx, ATTN_WIDTH), w_attn_o[l], gmlp_norm_g[l],
                             gmlp_ws[l], gmlp_bs[l], w_gmlp_o[l], conv_w[l], conv_b[l],
                             conv_norm_g[l], conv_norm_b[l], w_conv_o[l], w_out[l])
            xc = xc + gc1 * rms_norm(yc, mix_post_g[l])
            hc2 = modulate(rms_norm(xc, ffn_pre_g[l]), shc2, scc2)
            xc = xc + gc2 * rms_norm(sq_relu_mlp(hc2, w_ff1[l], w_ff2[l]), ffn_post_g[l])
    return x


DEPTH_2 = 1

HEAD_DIM_2 = 64
GDN_HEADS = 6
GDN_CONV = 4
GDN_CHUNK = 64
GDN_WIDTH = GDN_HEADS * HEAD_DIM_2
NSA_HEADS = 6
NSA_KV_HEADS = 2
NSA_GROUP = NSA_HEADS // NSA_KV_HEADS
NSA_WIDTH = NSA_HEADS * HEAD_DIM_2
NSA_KV_WIDTH = NSA_KV_HEADS * HEAD_DIM_2
CMP_LEN = 32
CMP_STRIDE = 16
CMP_HIDDEN = 256
SEL_BLOCK = 64
SEL_TOPK = 16
WINDOW = 512
FORCED_SCORE = 1e4
POOL_WINDOWS = (2, 4, 8, 16)
POOL_GROUP_DIM = 64
POOL_WIDTH = 4 * POOL_GROUP_DIM
D_MIX = GDN_WIDTH + NSA_WIDTH + POOL_WIDTH
IN_SPLITS = (3 * GDN_WIDTH, GDN_WIDTH, GDN_HEADS, GDN_HEADS, NSA_WIDTH, 6 * NSA_KV_WIDTH, 3 * NSA_HEADS, POOL_WIDTH)
D_IN = 3 * GDN_WIDTH + GDN_WIDTH + GDN_HEADS + GDN_HEADS + NSA_WIDTH + 6 * NSA_KV_WIDTH + 3 * NSA_HEADS + POOL_WIDTH
D_FF_2 = 4 * D_MODEL


def rms_norm_2(x, g):
    xf = x.astype(jnp.float32)
    return (xf * lax.rsqrt(jnp.mean(xf * xf, axis=-1, keepdims=True) + EPS) * g).astype(x.dtype)

def l2norm(x):
    xf = x.astype(jnp.float32)
    return xf * lax.rsqrt(jnp.sum(xf * xf, axis=-1, keepdims=True) + EPS)

def masked_softmax(s, mask):
    s = jnp.where(mask, s.astype(jnp.float32), -1e30)
    return jax.nn.softmax(s, axis=-1) * mask

def split_columns(proj):
    offs = []
    acc = 0
    for s in IN_SPLITS[:-1]:
        acc += s
        offs.append(acc)
    return jnp.split(proj, offs, axis=-1)

def causal_conv(x, w):
    T = x.shape[1]
    K = w.shape[0]
    xp = jnp.pad(x, ((0, 0), (K - 1, 0), (0, 0)))
    return sum(xp[:, k:k + T] * w[k] for k in range(K))

def gated_delta_rule(q, k, v, beta, g):
    B, T, H, Dk = q.shape
    Dv = v.shape[-1]
    C = GDN_CHUNK
    N = T // C
    f32 = jnp.float32

    def chunks(a):
        a = a.astype(f32).reshape((B, N, C, H) + a.shape[3:])
        return jnp.moveaxis(a, 3, 1)

    q, k, v, beta, g = map(chunks, (q, k, v, beta, g))
    q = q * Dk ** -0.5
    gc = jnp.cumsum(g, axis=-1)
    causal = jnp.tril(jnp.ones((C, C), bool))
    strict = jnp.tril(jnp.ones((C, C), bool), -1)
    decay = jnp.exp(jnp.where(causal, gc[..., :, None] - gc[..., None, :], -jnp.inf))
    k_beta = k * beta[..., None]
    L = jnp.where(strict, jnp.einsum('bhncd,bhnsd->bhncs', k_beta, k) * decay, 0.0)
    A = jnp.eye(C, dtype=f32) + L
    u = lax.linalg.triangular_solve(A, v * beta[..., None], left_side=True, lower=True, unit_diagonal=True)
    w = lax.linalg.triangular_solve(A, k_beta * jnp.exp(gc)[..., None], left_side=True, lower=True, unit_diagonal=True)
    qk = jnp.einsum('bhncd,bhnsd->bhncs', q, k) * decay
    q_dec = q * jnp.exp(gc)[..., None]
    k_dec = k * jnp.exp(gc[..., -1:] - gc)[..., None]
    g_last = jnp.exp(gc[..., -1])

    def step(S, xs):
        u_i, w_i, qk_i, qd_i, kd_i, gl_i = xs
        v_new = u_i - jnp.einsum('bhcd,bhde->bhce', w_i, S)
        o = jnp.einsum('bhcd,bhde->bhce', qd_i, S) + jnp.einsum('bhcs,bhse->bhce', qk_i, v_new)
        S = S * gl_i[..., None, None] + jnp.einsum('bhcd,bhce->bhde', kd_i, v_new)
        return S, o

    xs = tuple(jnp.moveaxis(a, 2, 0) for a in (u, w, qk, q_dec, k_dec, g_last))
    S0 = jnp.zeros((B, H, Dk, Dv), f32)
    _, o = lax.scan(step, S0, xs)
    return jnp.transpose(o, (1, 0, 3, 2, 4)).reshape(B, T, H, Dv)

def gdn_mixer(qkv, z, b, a, conv_w, a_log, dt_bias, norm_g):
    B, T, _ = qkv.shape
    qkv = jax.nn.silu(causal_conv(qkv, conv_w))
    q, k, v = jnp.split(qkv, 3, axis=-1)
    heads = lambda t: t.reshape(B, T, GDN_HEADS, HEAD_DIM_2)
    q, k, v = l2norm(heads(q)), l2norm(heads(k)), heads(v)
    beta = jax.nn.sigmoid(b.astype(jnp.float32))
    g = -jnp.exp(a_log.astype(jnp.float32)) * jax.nn.softplus(a.astype(jnp.float32) + dt_bias)
    o = gated_delta_rule(q, k, v, beta, g)
    o = rms_norm_2(o, norm_g) * jax.nn.silu(heads(z).astype(jnp.float32))
    return o.reshape(B, T, GDN_WIDTH).astype(qkv.dtype)

def compress(x, pos, w1, w2):
    B, T, H, D = x.shape
    R = CMP_LEN // CMP_STRIDE
    Nr = T // CMP_STRIDE
    r = x.reshape(B, Nr, CMP_STRIDE, H, D)
    blocks = jnp.concatenate([r[:, i:Nr - R + 1 + i] for i in range(R)], axis=2)
    blocks = blocks + pos[None, None, :, None, :]
    Nc = blocks.shape[1]
    flat = blocks.transpose(0, 1, 3, 2, 4).reshape(B, Nc, H, CMP_LEN * D)
    out = jax.nn.silu(flat @ w1) @ w2
    return out.transpose(0, 2, 1, 3)

def cmp_to_sel(p):
    R = SEL_BLOCK // CMP_STRIDE
    P = CMP_LEN // CMP_STRIDE - 1
    Ns = (p.shape[-1] + P) // R
    pp = jnp.pad(p, [(0, 0)] * (p.ndim - 1) + [(P, P)])
    return sum(lax.slice_in_dim(pp, o, o + R * (Ns - 1) + 1, stride=R, axis=-1) for o in range(R + P))

def nsa_mixer(q, kv, gate_logits, q_norm, k_norm, cmp_pos, cmp_w1, cmp_w2):
    B, T, _ = q.shape
    Hkv, G, Dh = NSA_KV_HEADS, NSA_GROUP, HEAD_DIM_2
    out_dtype = q.dtype
    scale = Dh ** -0.5
    q = rms_norm_2(q.reshape(B, T, NSA_HEADS, Dh), q_norm)
    q = q.reshape(B, T, Hkv, G, Dh).transpose(0, 2, 3, 1, 4)
    kc, vc, ks, vs, kw, vw = [t.reshape(B, T, Hkv, Dh) for t in jnp.split(kv, 6, axis=-1)]
    kc = rms_norm_2(compress(kc, cmp_pos[0], cmp_w1[0], cmp_w2[0]), k_norm[0])
    vc = compress(vc, cmp_pos[1], cmp_w1[1], cmp_w2[1])
    Nc = kc.shape[2]
    Ns = T // SEL_BLOCK
    K_SEL = min(SEL_TOPK, Ns)
    ks = rms_norm_2(ks, k_norm[1]).transpose(0, 2, 1, 3).reshape(B, Hkv, Ns, SEL_BLOCK, Dh)
    vs = vs.transpose(0, 2, 1, 3).reshape(B, Hkv, Ns, SEL_BLOCK, Dh)
    pad = ((0, 0), (0, 0), (WINDOW, 0), (0, 0))
    kw = jnp.pad(rms_norm_2(kw, k_norm[2]).transpose(0, 2, 1, 3), pad)
    vw = jnp.pad(vw.transpose(0, 2, 1, 3), pad)
    gates = jax.nn.sigmoid(gate_logits.astype(jnp.float32)).reshape(B, T, Hkv, G, 3).transpose(0, 2, 3, 1, 4)
    cmp_end = jnp.arange(Nc) * CMP_STRIDE + CMP_LEN - 1
    blk = jnp.arange(Ns)
    bidx = jnp.arange(B)[:, None, None, None]
    hidx = jnp.arange(Hkv)[None, :, None, None]

    def block(i):
        t0 = i * Q_BLOCK
        pos = t0 + jnp.arange(Q_BLOCK)
        qb = lax.dynamic_slice_in_dim(q, t0, Q_BLOCK, axis=3) * scale
        gb = lax.dynamic_slice_in_dim(gates, t0, Q_BLOCK, axis=3)
        s = jnp.einsum('bhgqd,bhcd->bhgqc', qb, kc)
        p_c = masked_softmax(s, cmp_end[None, :] <= pos[:, None])
        o_c = jnp.einsum('bhgqc,bhcd->bhgqd', p_c, vc)
        imp = cmp_to_sel(p_c.sum(axis=2))
        cur = pos // SEL_BLOCK
        forced = (blk[None] == 0) | (blk[None] == cur[:, None]) | (blk[None] == cur[:, None] - 1)
        valid = blk[None] * SEL_BLOCK <= pos[:, None]
        imp = jnp.where(forced, FORCED_SCORE, jnp.where(valid, imp, -1.0))
        _, idx = lax.top_k(imp, K_SEL)
        ksel = ks[bidx, hidx, idx]
        vsel = vs[bidx, hidx, idx].reshape(B, Hkv, Q_BLOCK, K_SEL * SEL_BLOCK, Dh)
        s = jnp.einsum('bhgqd,bhqksd->bhgqks', qb, ksel).reshape(B, Hkv, G, Q_BLOCK, K_SEL * SEL_BLOCK)
        key_pos = idx[..., None] * SEL_BLOCK + jnp.arange(SEL_BLOCK)
        mask_s = (key_pos <= pos[:, None, None]).reshape(B, Hkv, 1, Q_BLOCK, K_SEL * SEL_BLOCK)
        o_s = jnp.einsum('bhgqn,bhqnd->bhgqd', masked_softmax(s, mask_s), vsel)
        kwb = lax.dynamic_slice_in_dim(kw, t0, Q_BLOCK + WINDOW, axis=2)
        vwb = lax.dynamic_slice_in_dim(vw, t0, Q_BLOCK + WINDOW, axis=2)
        kpos = t0 - WINDOW + jnp.arange(Q_BLOCK + WINDOW)
        mask_w = (kpos[None] <= pos[:, None]) & (kpos[None] > pos[:, None] - WINDOW) & (kpos[None] >= 0)
        s = jnp.einsum('bhgqd,bhkd->bhgqk', qb, kwb)
        o_w = jnp.einsum('bhgqk,bhkd->bhgqd', masked_softmax(s, mask_w), vwb)
        return gb[..., 0:1] * o_c + gb[..., 1:2] * o_s + gb[..., 2:3] * o_w

    out = lax.map(block, jnp.arange(T // Q_BLOCK))
    return out.transpose(1, 0, 4, 2, 3, 5).reshape(B, T, NSA_WIDTH).astype(out_dtype)

def pool_mixer(u, pool_w, pool_scale):
    B, T, _ = u.shape
    uf = u.astype(jnp.float32)
    c = jnp.pad(jnp.cumsum(uf, axis=1), ((0, 0), (1, 0), (0, 0)))
    t1 = jnp.arange(1, T + 1, dtype=jnp.float32)
    outs = []
    for gi, w in enumerate(POOL_WINDOWS):
        sl = slice(gi * POOL_GROUP_DIM, (gi + 1) * POOL_GROUP_DIM)
        cg = c[..., sl]
        cg_lag = jnp.pad(cg, ((0, 0), (w - 1, 0), (0, 0)))[:, :T]
        mean = (cg[:, 1:] - cg_lag) / jnp.minimum(t1, float(w))[None, :, None]
        outs.append(jnp.einsum('btc,cd->btd', mean - uf[..., sl], pool_w[gi]))
    return (jnp.concatenate(outs, axis=-1) * pool_scale).astype(u.dtype)

def second_inputs(seed: int = 0) -> dict:
    key = jax.random.key(seed)
    keys = jax.random.split(key, 20)
    nrm = lambda k, shape, s: jax.random.normal(k, shape, jnp.float32) * s
    L = DEPTH_2
    x = nrm(keys[0], (BATCH, SEQ, D_MODEL), 1.0)
    norm_mix = 1.0 + nrm(keys[1], (L, D_MODEL), 0.02)
    w_in = nrm(keys[2], (L, D_MODEL, D_IN), D_MODEL ** -0.5)
    conv_w = nrm(keys[3], (L, GDN_CONV, 3 * GDN_WIDTH), GDN_CONV ** -0.5)
    a_log = jnp.log(jax.random.uniform(keys[4], (L, GDN_HEADS), jnp.float32, 1.0, 16.0))
    dt = jnp.exp(jax.random.uniform(keys[5], (L, GDN_HEADS), jnp.float32, math.log(1e-3), math.log(1e-1)))
    dt_bias = dt + jnp.log(-jnp.expm1(-dt))
    gdn_norm = 1.0 + nrm(keys[6], (L, HEAD_DIM_2), 0.02)
    nsa_q_norm = 1.0 + nrm(keys[7], (L, HEAD_DIM_2), 0.02)
    nsa_k_norm = 1.0 + nrm(keys[8], (L, 3, HEAD_DIM_2), 0.02)
    cmp_pos = nrm(keys[9], (L, 2, CMP_LEN, HEAD_DIM_2), 0.1)
    cmp_w1 = nrm(keys[10], (L, 2, CMP_LEN * HEAD_DIM_2, CMP_HIDDEN), (CMP_LEN * HEAD_DIM_2) ** -0.5)
    cmp_w2 = nrm(keys[11], (L, 2, CMP_HIDDEN, HEAD_DIM_2), CMP_HIDDEN ** -0.5)
    pool_w = nrm(keys[12], (L, len(POOL_WINDOWS), POOL_GROUP_DIM, POOL_GROUP_DIM), POOL_GROUP_DIM ** -0.5)
    pool_scale = 1.0 + nrm(keys[13], (L, POOL_WIDTH), 0.1)
    w_out = nrm(keys[14], (L, D_MIX, D_MODEL), (2 * DEPTH_2 * D_MIX) ** -0.5)
    norm_ffn = 1.0 + nrm(keys[15], (L, D_MODEL), 0.02)
    w_ffn1 = nrm(keys[16], (L, D_MODEL, D_FF_2), D_MODEL ** -0.5)
    w_ffn2 = nrm(keys[17], (L, D_FF_2, D_MODEL), (2 * DEPTH_2 * D_FF_2) ** -0.5)
    return {"x": x, "norm_mix": norm_mix, "w_in": w_in, "conv_w": conv_w, "a_log": a_log, "dt_bias": dt_bias,
            "gdn_norm": gdn_norm, "nsa_q_norm": nsa_q_norm, "nsa_k_norm": nsa_k_norm, "cmp_pos": cmp_pos,
            "cmp_w1": cmp_w1, "cmp_w2": cmp_w2, "pool_w": pool_w, "pool_scale": pool_scale, "w_out": w_out,
            "norm_ffn": norm_ffn, "w_ffn1": w_ffn1, "w_ffn2": w_ffn2}

def second_block(x, norm_mix, w_in, conv_w, a_log, dt_bias, gdn_norm, nsa_q_norm, nsa_k_norm, cmp_pos,
              cmp_w1, cmp_w2, pool_w, pool_scale, w_out, norm_ffn, w_ffn1, w_ffn2):
    for l in range(DEPTH_2):
        h = rms_norm_2(x, norm_mix[l])
        proj = h @ w_in[l]
        qkv_a, z_a, b_a, a_a, q_b, kv_b, gate_b, u_c = split_columns(proj)
        y_a = gdn_mixer(qkv_a, z_a, b_a, a_a, conv_w[l], a_log[l], dt_bias[l], gdn_norm[l])
        y_b = nsa_mixer(q_b, kv_b, gate_b, nsa_q_norm[l], nsa_k_norm[l], cmp_pos[l], cmp_w1[l], cmp_w2[l])
        y_c = pool_mixer(u_c, pool_w[l], pool_scale[l])
        y = jnp.concatenate([y_a.astype(x.dtype), y_b.astype(x.dtype), y_c.astype(x.dtype)], axis=-1)
        x = x + y @ w_out[l]
        h = rms_norm_2(x, norm_ffn[l])
        x = x + jnp.square(jax.nn.relu(h @ w_ffn1[l])) @ w_ffn2[l]
    return x


def setup_inputs(seed=0):
    out = dict(first_inputs(seed))
    for name, value in second_inputs(seed + 1).items():
        if name != "x":
            out[name + "_2"] = value
    return out


def reference(
    x, c, ctx, c_ctx, ada_w, ada_b, mix_pre_g, mix_post_g, w_in, q_norm_g, k_norm_g, w_attn_o,
    gmlp_norm_g, gmlp_ws, gmlp_bs, w_gmlp_o, conv_w, conv_b, conv_norm_g, conv_norm_b, w_conv_o,
    w_out, ffn_pre_g, ffn_post_g, w_ff1, w_ff2, norm_mix_2, w_in_2, conv_w_2, a_log_2,
    dt_bias_2, gdn_norm_2, nsa_q_norm_2, nsa_k_norm_2, cmp_pos_2, cmp_w1_2, cmp_w2_2, pool_w_2,
    pool_scale_2, w_out_2, norm_ffn_2, w_ffn1_2, w_ffn2_2,
):
    x = first_block(
        x, c, ctx, c_ctx, ada_w, ada_b, mix_pre_g, mix_post_g, w_in, q_norm_g, k_norm_g,
        w_attn_o, gmlp_norm_g, gmlp_ws, gmlp_bs, w_gmlp_o, conv_w, conv_b, conv_norm_g,
        conv_norm_b, w_conv_o, w_out, ffn_pre_g, ffn_post_g, w_ff1, w_ff2,
    )
    return second_block(
        x, norm_mix_2, w_in_2, conv_w_2, a_log_2, dt_bias_2, gdn_norm_2, nsa_q_norm_2,
        nsa_k_norm_2, cmp_pos_2, cmp_w1_2, cmp_w2_2, pool_w_2, pool_scale_2, w_out_2,
        norm_ffn_2, w_ffn1_2, w_ffn2_2,
    )


_drawn_inputs = setup_inputs


def setup_inputs(seed=0):
    import zlib

    import numpy as np

    out = dict(_drawn_inputs(seed))
    spreads = {}
    factors = {'ctx': 4.208,
     'q_norm_g': 8.0,
     'k_norm_g': 8.0,
     'conv_b': 7.147,
     'conv_norm_b': 8.0,
     'norm_mix_2': 5.479,
     'gdn_norm_2': 8.0,
     'nsa_q_norm_2': 8.0,
     'nsa_k_norm_2': 8.0,
     'cmp_pos_2': 6.276,
     'norm_ffn_2': 4.411}
    for name, (base, spread) in spreads.items():
        noise = np.random.default_rng([zlib.crc32(name.encode()), seed]).standard_normal(out[name].shape)
        drawn = base * np.exp(spread * noise) if base else spread * noise
        out[name] = __import__('jax').numpy.asarray(drawn.astype(out[name].dtype))
    for name, factor in factors.items():
        out[name] = (out[name] * factor).astype(out[name].dtype)
    return out
```

```python
from contextlib import ExitStack

import numpy as np

import concourse.bass as bass
from concourse import mybir

F32 = mybir.dt.float32
ALU = mybir.AluOpType
ACT = mybir.ActivationFunctionType
AX = mybir.AxisListType

P = 128
DM = 1024
KT = DM // P
TOK, CTX = 512, 256
NALL = TOK + CTX
MT, CT = TOK // P, CTX // P
AT = MT + CT
DEPTH = 2
HEADS, KVH, HD = 8, 2, 128
CONVK = 31
PAD = CONVK // 2
COLS = 512
NVEC = CONVK + 6
GW = (TOK + 2 * PAD) + (CTX + 2 * PAD)
K_OFF, GU_OFF, GV_OFF, CG_OFF, GATE_OFF = 1024, 1536, 2560, 3584, 5632
EPS = 1e-6


class Signal:

    def __init__(self, sem, per_run):
        self.sem, self.per_run = sem, per_run

    def at(self, run, n):
        return self.sem, sum(self.per_run[:run]) + n


class Chain:

    def __init__(self, engine, sem):
        self.engine, self.sem, self.n, self.turn, self.per_turn = engine, sem, 0, 0, 0

    def link(self, instruction):
        instruction.then_inc(self.sem, 1)
        self.n += 1
        self.engine.wait_ge(self.sem, self.n + self.turn)

    def note(self, instruction):
        instruction.then_inc(self.sem, 1)
        self.n += 1

    def meet(self, back=0):
        self.engine.wait_ge(self.sem, self.n - back + self.turn)

    def enter(self, i, steps):
        self.turn, self.entry, self.steps = i * steps, self.n, steps

    def leave(self, turns):
        assert self.n - self.entry == self.steps, (self.n - self.entry, self.steps)
        self.turn, self.n = 0, self.entry + turns * self.steps


def build_program(nc, t, out):
    ctx = ExitStack()
    with ctx:
        def sbuf(name, shape, dt=F32):
            return ctx.enter_context(nc.sbuf_tensor("sb_" + name, shape, dt))

        def semaphore(name):
            return ctx.enter_context(nc.semaphore(name))

        def signal(name, *per_run):
            return Signal(semaphore(name), per_run)

        x = sbuf("x", [P, AT, DM])
        ht = sbuf("ht", [P, KT, NALL])
        ring = sbuf("ring", [P, 2, KT, COLS])
        ra = sbuf("ra", [P, KT * NALL])
        rb = sbuf("rb", [P, KT * NALL])
        kv = sbuf("kv", [P, AT, COLS])
        kt = sbuf("kt", [P, KVH, NALL])
        rc = sbuf("rc", [P, KT * NALL + (KT + 1) * GW])
        RD = KT * NALL
        ident = sbuf("ident", [P, P])
        rope = sbuf("rope", [P, MT, HD])
        vec = sbuf("vec", [P, KT, NVEC])
        modc = sbuf("modc", [P, 4, KT, 2])
        fused = sbuf("fused", [P, 2, KT, 2])
        gains = sbuf("gains", [P, 2, HD])
        ccol = sbuf("ccol", [P, KT, 2])
        ss = sbuf("ss", [P, 84])
        rstd = sbuf("rstd", [P, 84])
        ones = sbuf("ones", [P, P])
        eps = sbuf("eps", [P, 1])
        red = sbuf("red", [P, 10])
        psum = ctx.enter_context(nc.psum_tensor("psum", [P, 8 * 512], F32))
        mods = nc.dram_tensor("mods", (DEPTH, 2, 6 * DM), F32, kind="Internal").ap()

        def bank(b, n=512, at=0):
            return psum[:, b * 512 + at:b * 512 + at + n]

        q_cm = ra[:, :].rearrange("p (k n) -> p k n", k=KT)
        y_tm = ra[:, :].rearrange("p (t d) -> p t d", t=AT)
        q_tm = rb[:, :].rearrange("p (b t d) -> p b t d", b=2, t=AT)
        acc = rb[:, :].rearrange("p (k n) -> p k n", k=KT)
        xn_b = rb[:, :].rearrange("p (t d) -> p t d", t=AT)
        u_cm = rc[:, 0:RD].rearrange("p (k n) -> p k n", k=KT)
        gv_tm = rc[:, RD:2 * RD].rearrange("p (t d) -> p t d", t=AT)
        hid = rc[:, 0:2 * RD].rearrange("p (k n) -> p k n", k=2 * KT)
        PT = rb[:, 0:AT * TOK].rearrange("p (k n) -> p k n", k=AT)
        probs = [rb[:, 3072 + 768 * i:3072 + 768 * (i + 1)] for i in range(3)]
        ws_raw = rb[:, 0:512].rearrange("p (g q) -> p g q", g=4)
        ws_t = rb[:, 1024:1536].rearrange("p (g q) -> p g q", g=4)
        bs_row = rb[:, 512:1024].rearrange("p (g q) -> p g q", g=4)
        gate = kv[:, 0:4, :].rearrange("p a b -> p (a b)")
        gate4 = kv[:, :, :].rearrange("p a b -> p (a b)").rearrange("p (j n) -> p j n", j=4)
        branch = kt[:, :, :]

        SN, SG, SY, SQ = 0, 6, 12, 24

        def conv_slot(j, start, n):
            return rc[:, bass.ds(RD + j * GW + start, n)]

        NT = [AT, MT]
        s_const_in = signal("const_in", 16 * 2)
        s_x_in = signal("x_in", 16 * 2)
        s_c_in = signal("c_in", 16 * 2)
        s_adab_in = signal("adab_in", *[32] * DEPTH)
        s_vecs_in = signal("vecs_in", *[16 * 7] * DEPTH)
        s_gain_in = signal("gain_in", *[32] * DEPTH)
        s_ws_in = signal("ws_in", *[32] * DEPTH)
        s_post_in = signal("post_in", *[48] * (2 * DEPTH))
        s_mods_out = signal("mods_out", *[16] * DEPTH)
        s_out_stored = signal("out_stored", 16)
        wl = [semaphore("w_loaded0"), semaphore("w_loaded1")]
        s_consts = signal("consts", 1)
        s_c_silu = signal("c_silu", 1)
        s_c_turned = signal("c_turned", 1)
        s_c_ready = signal("c_ready", 1)
        s_ada_ps = signal("ada_ps", *[12] * DEPTH)
        s_ada_row = signal("ada_row", *[12] * DEPTH)
        s_cols_ps = signal("cols_ps", *[2] * DEPTH)
        s_cols_ready = signal("cols_ready", *[1] * DEPTH)
        NORM_T = [AT, AT, AT, MT, MT, MT]
        s_norm_rms = signal("norm_rms", *[1] * 6)
        s_norm_xn = signal("norm_xn", *NORM_T)
        s_norm_ps = signal("norm_ps", *[KT] * 6)
        s_norm_ht = signal("norm_ht", *[KT] * 6)
        QT = [AT * 3, MT * 2 + AT]
        s_qkv_ps = signal("qkv_ps", *QT)
        s_qkv_sb = signal("qkv_sb", *QT)
        s_qkv_red = signal("qkv_red", *QT)
        s_qkv_rms = signal("qkv_rms", *[1] * DEPTH)
        s_qkv_roped = signal("qkv_roped", *[1] * DEPTH)
        s_gu_ps = signal("gu_ps", *[KT] * DEPTH)
        s_gu_sb = signal("gu_sb", *[KT] * DEPTH)
        s_gv_ps = signal("gv_ps", *[2 * n for n in NT])
        s_gv_sb = signal("gv_sb", *[2 * n for n in NT])
        s_gv_rms = signal("gv_rms", *[1] * DEPTH)
        s_gv_ready = signal("gv_ready", *[1] * DEPTH)
        QH = [HEADS * 1 + KVH] * DEPTH
        s_qk_ps = signal("qk_ps", *QH)
        s_qk_cm = signal("qk_cm", *QH)
        UN = [HEADS * (MT + CT), HEADS * MT]
        OH = [2 * HEADS, HEADS]
        s_att_s = signal("att_s", *UN)
        s_att_mx = signal("att_mx", *UN)
        s_att_e = signal("att_e", *UN)
        s_att_p = signal("att_p", *UN)
        s_att_t = signal("att_t", *UN)
        s_att_pt = signal("att_pt", *UN)
        s_att_o = signal("att_o", *OH)
        s_att_sb = signal("att_sb", *OH)
        s_ws_ps = signal("ws_ps", *[1] * DEPTH)
        s_ws_ready = signal("ws_ready", *[1] * DEPTH)
        s_sv_ps = signal("sv_ps", *[KT] * DEPTH)
        s_sv_ready = signal("sv_ready", *[KT] * DEPTH)
        s_cgb_ps = signal("cgb_ps", *[KT] * DEPTH)
        s_cgb_sb = signal("cgb_sb", *[KT] * DEPTH)
        s_cga_ps = signal("cga_ps", *[KT] * DEPTH)
        s_glu_ready = signal("glu_ready", *[KT] * DEPTH)
        s_pads = signal("pads", *[1] * DEPTH)
        BR = [KT] * (3 * DEPTH)
        s_bg_ps = signal("bg_ps", *BR)
        s_bg_sb = signal("bg_sb", *BR)
        s_bo_ps = signal("bo_ps", *BR)
        s_bo_sb = signal("bo_sb", *BR)
        s_merged = signal("merged", *BR)
        s_conv_ready = signal("conv_ready", *[KT] * DEPTH)
        s_mean_ps = signal("mean_ps", *[1] * DEPTH)
        s_mean_sb = signal("mean_sb", *[1] * DEPTH)
        s_centred = signal("centred", *[KT] * DEPTH)
        s_squared = signal("squared", *[KT] * DEPTH)
        s_var_ps = signal("var_ps", *[1] * DEPTH)
        s_std_sb = signal("std_sb", *[1] * DEPTH)
        s_normed = signal("normed", *[KT] * DEPTH)
        s_conv_cm = signal("conv_cm", *[KT] * DEPTH)
        s_y_ps = signal("y_ps", *[2 * n for n in NT])
        s_y_sb = signal("y_sb", *[2 * n for n in NT])
        s_y_sq = signal("y_sq", *[NT[r // 2] for r in range(2 * DEPTH)])
        s_post_rms = signal("post_rms", *[1] * (2 * DEPTH))
        s_x_added = signal("x_added", *[NT[r // 2] - 1 for r in range(2 * DEPTH)])
        s_x_ready = signal("x_ready", *[1] * (2 * DEPTH))
        s_hid_ps = signal("hid_ps", *[4 * KT] * (DEPTH + 1))
        s_hid_relu = signal("hid_relu", *[4 * KT] * (DEPTH + 1))
        s_hid_ready = signal("hid_ready", *[4 * KT] * (DEPTH + 1))
        FF = [4 * (1 + n) for n in NT + [MT]]
        s_ff_ps = signal("ff_ps", *FF)
        s_ff_copied = signal("ff_copied", *[2 * n for n in NT])
        s_ff_added = signal("ff_added", *[2 * n for n in NT], 4 * MT)
        chain_sem = {n: semaphore(f"{n}_order") for n in ("act", "dve", "pool")}

        def cols(w, c0, r0=0):
            v = w[r0:r0 + DM, :].rearrange("(t p) n -> p t n", p=P)
            return lambda i: v[:, :, bass.ds(c0 + i * COLS, COLS)]

        CH2 = 64
        NCH = TOK // CH2
        H2, D2, KV2 = 6, 64, 2
        QKV = 3 * H2 * D2
        CTAPS = 4
        O_Z, O_B, O_A, O_Q, O_KV, O_GATE, O_U = 0, 384, 390, 396, 780, 1548, 1566
        PJW = 1822
        PJ_END = MT * PJW
        XW = TOK + CTAPS - 1
        NSAH = 6
        assert TOK // 64 <= 16, "every selection block is among the top 16, so selection keeps them all"
        assert TOK <= 512, "the window covers every earlier token"
        KEYS = 32

        hflat = ht[:, :, :].rearrange("p a b -> p (a b)")
        kvflat = kv[:, :, :].rearrange("p a b -> p (a b)")
        ktflat = kt[:, :, :].rearrange("p a b -> p (a b)")
        xtail = x[:, MT:AT, :].rearrange("p a b -> p (a b)")
        vflat = vec[:, :, :].rearrange("p a b -> p (a b)")
        rows2 = rope[:, :, :].rearrange("p a b -> p (a b)")
        gflat = gains[:, :, :].rearrange("p a b -> p (a b)")
        conv_in = rc[:, PJ_END:PJ_END + 9 * XW].rearrange("p (c n) -> p c n", c=9)
        conv_out = ra[:, 0:9 * TOK].rearrange("p (c n) -> p c n", c=9)
        pj = rc[:, 0:PJ_END].rearrange("p (t n) -> p t n", t=MT)
        qkv2 = rb[:, 0:MT * QKV].rearrange("p (t n) -> p t n", t=MT)
        kbe = rb[:, MT * QKV:MT * QKV + 1536].rearrange("p (t n) -> p t n", t=MT)
        kdec = ktflat.rearrange("p (t n) -> p t n", t=MT)
        qT = hflat[0:D2, 0:3072].rearrange("p (h n) -> p h n", h=H2)
        kT = hflat[0:D2, 3072:6144].rearrange("p (h n) -> p h n", h=H2)

        def by_unit(ap, n=8):
            return ap.rearrange("p (u h n) -> p u h n", u=n, h=3)

        xi, xit = by_unit(ra[:, 0:3072]), by_unit(ra[:, 3072:6144])
        lt, qkt = by_unit(rc[:, PJ_END:PJ_END + 3072]), by_unit(rc[:, PJ_END + 3072:PJ_END + 6144])
        lm = by_unit(kvflat)
        bt = by_unit(ktflat, 4)
        MASKS = ("prefix", "far", "near", "pair", "pair_t", "l2", "l4", "l8", "l16", "l32", "same", "first", "last")
        mask = {m: xtail[:, i * P:(i + 1) * P] for i, m in enumerate(MASKS)}
        levels = xtail[:, 5 * P:10 * P].rearrange("p (m n) -> p m n", m=5)
        NSM = 12
        small = xtail[:, 13 * P:13 * P + NSM * 24].rearrange("p (r n) -> p r n", r=NSM)
        XA, AB, EY, UU, G, GC, NGC, KD, EGC, EKD, LN_, BETA = range(NSM)
        state = sbuf("state", [D2, H2 * D2])
        glast = sbuf("glast", [P, 2, 24])
        R_AL, R_DT, R_GN, R_QN, R_KN, R_CM = 0, 6, 16, 80, 144, 336
        cneg = gflat[:, 0:128].rearrange("p (t n) -> p t n", t=MT)
        cmask = gflat[:, 128:256].rearrange("p (t n) -> p t n", t=MT)
        hT = hflat[0:D2, :].rearrange("p (h n) -> p h n", h=12)
        vcT = kvflat[0:D2, 0:1024].rearrange("p (h n) -> p h n", h=2)
        kp = ra[0:D2, 0:4096].rearrange("p (s t h n) -> p s t h n", s=2, t=32, h=2)
        hidc = ra[0:D2, 4096:4608].rearrange("p (s n) -> p s n", s=2)
        hidT = ra[:, 4608:4864].rearrange("p (s k n) -> p s k n", s=2, k=2)
        ck = ra[0:32, 4864:5120].rearrange("p (j d) -> p j d", j=4)
        ckT = ra[0:D2, 5120:5184].rearrange("p (h n) -> p h n", h=2)
        csc = ra[:, 5184:5376]
        ctmp = ra[:, 5376:5760]
        pcT = ktflat[0:32, 0:768].rearrange("p (h n) -> p h n", h=6)
        w2c = xtail[:, 0:256].rearrange("p (s k d) -> p s k d", s=2, k=2)
        pw = xtail[0:D2, 256:512].rearrange("p (g d) -> p g d", g=4)
        nprobs = [rb[:, 512 * i:512 * (i + 1)] for i in range(3)]
        npt = [rb[:, 1536 + 512 * i:2048 + 512 * i].rearrange("p (k n) -> p k n", k=MT) for i in range(2)]
        oacc = rb[:, 2560:4096].rearrange("p (t n) -> p t n", t=MT)
        otmp = rb[:, 4096:4480]
        bands = rc[:, PJ_END:PJ_END + 1536].rearrange("p (m n) -> p m n", m=12)
        mT = ra[0:D2, 0:2048].rearrange("p (g n) -> p g n", g=4)
        ycm = hflat[:, 0:4096].rearrange("p (k n) -> p k n", k=KT)
        NUNITS = 48

        s_par2 = signal("par2", 16 * 14)
        s_col2_ps = signal("col2_ps", 1)
        s_col2_sb = signal("col2_sb", 1)
        s_cv_ps = signal("cv_ps", 9)
        s_cv_sb = signal("cv_sb", 9)
        s_pj_ps = signal("pj_ps", 16)
        s_pj_sb = signal("pj_sb", 16)
        s_cv_done = signal("cv_done", 9)
        s_cv_act = signal("cv_act", 9)
        s_tm_ps = signal("tm_ps", 9)
        s_tm_sb = signal("tm_sb", 9)
        s_sm_dve = signal("sm_dve", 16)
        s_sm_act = signal("sm_act", 16)
        s_gs_ps = signal("gs_ps", 1)
        s_h2_ps = signal("h2_ps", 18)
        s_h2_sb = signal("h2_sb", 18)
        s_dec_ps = signal("dec_ps", 8)
        s_dec_sb = signal("dec_sb", 8)
        s_lq = signal("lq", 8)
        s_lt_ps = signal("lt_ps", 8)
        s_lt_sb = signal("lt_sb", 8)
        s_x0 = signal("x0", 8)
        s_bt = signal("bt", 40)
        s_p1_ps = signal("p1_ps", 40)
        s_p1_sb = signal("p1_sb", 40)
        s_xx_ps = signal("xx_ps", 40)
        s_xx_sb = signal("xx_sb", 40)
        s_wu_ps = signal("wu_ps", 8)
        s_w_sb = signal("w_sb", 8)
        s_u_sb = signal("u_sb", 8)
        s_vs_ps = signal("vs_ps", 8)
        s_vn = signal("vn", 8)
        s_o2_ps = signal("o2_ps", 8)
        s_o2_sb = signal("o2_sb", 8)
        s_oi_sb = signal("oi_sb", 8)
        s_s_up = signal("s_up", 9)
        s_par3 = signal("par3", 16 * 3)
        s_nt_ps = signal("nt_ps", 14)
        s_nt_sb = signal("nt_sb", 14)
        s_kp = signal("kp", 2)
        s_hc_ps = signal("hc_ps", 2 * 2)
        s_hc_sb = signal("hc_sb", 1)
        s_hct_ps = signal("hct_ps", 1)
        s_hct_sb = signal("hct_sb", 1)
        s_ck_ps = signal("ck_ps", 1)
        s_ckt_ps = signal("ckt_ps", 1)
        s_ckt_sb = signal("ckt_sb", 1)
        s_cs_ps = signal("cs_ps", 4)
        s_cs_mx = signal("cs_mx", 4)
        s_cs_e = signal("cs_e", 4)
        s_cs_p = signal("cs_p", 4)
        s_ct_ps = signal("ct_ps", 4)
        s_ct_sb = signal("ct_sb", 4)
        s_co_ps = signal("co_ps", 4)
        s_ns_ps = signal("ns_ps", NUNITS)
        s_ns_mx = signal("ns_mx", NUNITS)
        s_ns_e = signal("ns_e", NUNITS)
        s_nt2_ps = signal("nt2_ps", NUNITS)
        s_nt2_sb = signal("nt2_sb", NUNITS)
        s_no_ps = signal("no_ps", 8)
        s_o_acc = signal("o_acc", 12)
        s_mt_ps = signal("mt_ps", 4)
        s_mt_sb = signal("mt_sb", 4)
        s_yc_ps = signal("yc_ps", 2)
        s_y_cm = signal("y_cm", 8)
        s_yt_ps = signal("yt_ps", 6)
        s_xw_ps = signal("xw_ps", 8)
        def bc(ap, n):
            return ap.unsqueeze(2).to_broadcast([ap.shape[0], ap.shape[1], n])

        def rep(ap, r):
            return ap.unsqueeze(1).to_broadcast([ap.shape[0], r, ap.shape[1]])

        def by_head(ap):
            return ap.rearrange("p (h d) -> p h d", d=D2)

        nsa = [(i, br, h) for i in range(MT) for br in (1, 2) for h in range(NSAH)]
        VOFF = {1: O_KV + 3 * 128, 2: O_KV + 5 * 128}

        def second_pool(pool, ch, load):
            pool.wait_ge(*s_x_ready.at(2 * DEPTH - 1, 1))
            load(rb[0:CTAPS, 0:QKV], t["conv_w_2"][0], s_par2)
            load(rb[0:1, QKV:QKV + DM], t["norm_mix_2"][0:1, :], s_par2)
            load(rb[1:2, QKV:QKV + DM], t["norm_ffn_2"][0:1, :], s_par2)
            load(rb[0:1, 2176:2432], t["pool_scale_2"][0:1, :], s_par2)
            load(rb[0:64, 2432:2496], t["cmp_pos_2"][0].rearrange("s t d -> (s t) d"), s_par2)
            load(rows2[:, R_AL:R_AL + 6], t["a_log_2"][0:1, :].to_broadcast([P, 6]), s_par2)
            load(rows2[:, R_DT:R_DT + 6], t["dt_bias_2"][0:1, :].to_broadcast([P, 6]), s_par2)
            load(rows2[:, R_GN:R_GN + D2], t["gdn_norm_2"][0:1, :].to_broadcast([P, D2]), s_par2)
            load(rows2[:, R_QN:R_QN + D2], t["nsa_q_norm_2"][0:1, :].to_broadcast([P, D2]), s_par2)
            load(rows2[:, R_KN:R_KN + 3 * D2].rearrange("p (a d) -> p a d", a=3),
                 t["nsa_k_norm_2"][0:1].to_broadcast([P, 3, D2]), s_par2)
            load(rows2[:, R_CM:R_CM + P], t["causal"], s_par2)
            load(cneg, t["cneg"].rearrange("(t p) n -> p t n", p=P), s_par2)
            load(cmask, t["cmask"].rearrange("(t p) n -> p t n", p=P), s_par2)
            load(xtail[:, 0:13 * P].rearrange("p (m n) -> p m n", m=13), t["masks"].rearrange("m p n -> p m n"),
                 s_par2)
            pool.wait_ge(*s_oi_sb.at(0, NCH))
            pool.wait_ge(*s_s_up.at(0, NCH + 1))
            for s in range(2):
                load(w2c[:, s, :, :], t["cmp_w2_2"][0, s].rearrange("(k p) d -> p k d", p=P), s_par3)
            load(pw, t["pool_w_2"][0].rearrange("g c d -> c g d"), s_par3)
            load(bands, t["bands"].rearrange("m p n -> p m n"), s_par3)

        def second_act(act, ch, fn, root, norm_sums, norm_drain):
            norm_sums(4, rc[:, 1024:2048])
            act.wait_ge(*s_col2_sb.at(0, 1))
            norm_drain(4, 0)
            for c in range(9):
                act.wait_ge(*s_cv_ps.at(0, c + 1))
                fn(conv_in[:, c, CTAPS - 1:XW], bank(2 * (c % 2))).then_inc(s_cv_sb.sem, 1)
            for g in range(16):
                b, i = divmod(g, 4)
                w = min(COLS, PJW - b * COLS)
                act.wait_ge(*s_pj_ps.at(0, g + 1))
                fn(pj[:, i, b * COLS:b * COLS + w], bank(4 + g % 4, w)).then_inc(s_pj_sb.sem, 1)
            for c in range(9):
                act.wait_ge(*s_cv_done.at(0, c + 1))
                fn(conv_out[:, c, :], conv_out[:, c, :], ACT.Silu).then_inc(s_cv_act.sem, 1)
            for c in range(9):
                act.wait_ge(*s_tm_ps.at(0, c + 1))
                fn(qkv2[:, :, c * P:(c + 1) * P], bank(4 + c % 4).rearrange("p (t n) -> p t n", t=MT)).then_inc(s_tm_sb.sem, 1)
            act.wait_ge(*s_sm_dve.at(0, 1))
            fn(small[:, EY, :], small[:, AB, :], ACT.Exp, scale=-1.0).then_inc(s_sm_act.sem, 1)
            fn(rows2[:, R_AL:R_AL + 6], rows2[:, R_AL:R_AL + 6], ACT.Exp).then_inc(s_sm_act.sem, 1)
            fn(small[:, BETA, :].rearrange("p (t h) -> p t h", t=MT), pj[:, :, O_B:O_B + 6], ACT.Sigmoid).then_inc(s_sm_act.sem, 1)
            act.wait_ge(*s_sm_dve.at(0, 2))
            fn(small[:, LN_, :], small[:, UU, :], ACT.Ln).then_inc(s_sm_act.sem, 1)
            act.wait_ge(*s_sm_dve.at(0, 4))
            fn(small[:, EGC, :], small[:, GC, :], ACT.Exp)
            fn(small[:, EKD, :], small[:, KD, :], ACT.Exp)
            fn(glast[:, :, :], glast[:, :, :], ACT.Exp).then_inc(s_sm_act.sem, 1)
            act.wait_ge(*s_sm_dve.at(0, 5))
            fn(ss[:, SQ:SQ + 48], ss[:, SQ:SQ + 48], ACT.Sqrt, bias=eps[:, 0:1]).then_inc(s_sm_act.sem, 1)

            def heads_out(g):
                act.wait_ge(*s_h2_ps.at(0, g + 1))
                dst = (qT, kT, qT)[g // 6][:, g % 6, :]
                fn(dst, bank(g % 4)[0:D2, :]).then_inc(s_h2_sb.sem, 1)

            for g in range(12):
                heads_out(g)
            for u in range(8):
                i, h0 = u // 2, 3 * (u % 2)
                act.wait_ge(*s_dec_ps.at(0, u + 1))
                for h in range(3):
                    at = 6 * i + h0 + h
                    fn(lm[:, u, h, :], bank(4 * (u % 2), P, h * P), ACT.Exp, scale=-1.0,
                       bias=small[:, GC, at:at + 1])
                    last = fn(qkt[:, u, h, :], bank(4 * (u % 2) + 1, P, h * P), ACT.Exp,
                              bias=small[:, NGC, at:at + 1])
                last.then_inc(s_dec_sb.sem, 1)
            for u in range(8):
                act.wait_ge(*s_lt_ps.at(0, u + 1))
                fn(lt[:, u, :, :], bank(u, 384).rearrange("p (h n) -> p h n", h=3)).then_inc(s_lt_sb.sem, 1)
            for g in range(12, 18):
                heads_out(g)
            with act.Fori(0, 5) as level:
                for u in range(8):
                    act.wait_ge(*s_p1_ps.at(0, 8 * level + u + 1))
                    fn(lm[:, u, :, :], bank(u % 2, 384).rearrange("p (h n) -> p h n", h=3)).then_inc(s_p1_sb.sem, 1)
            for u in range(8):
                i, h0 = u // 2, 3 * (u % 2)
                act.wait_ge(*s_wu_ps.at(0, u + 1))
                fn(kT[:, h0:h0 + 3, i * P:(i + 1) * P],
                       bank(2 * (u % 2), 384)[0:D2, :].rearrange("p (h n) -> p h n", h=3)).then_inc(s_w_sb.sem, 1)
            for c in range(NCH):
                i, r = c // 2, slice(CH2 * (c % 2), CH2 * (c % 2) + CH2)
                act.wait_ge(*s_o2_ps.at(0, c + 1))
                fn(qkv2[r, i, 0:384], bank(1 + c % 2, 384)[r, :]).then_inc(s_o2_sb.sem, 1)
            act.wait_ge(*s_sm_dve.at(0, 6))
            fn(ss[:, SQ:SQ + 40], ss[:, SQ:SQ + 40], ACT.Sqrt, scale=1.0 / D2, bias=eps[:, 0:1]).then_inc(s_sm_act.sem, 1)
            for g in range(14):
                act.wait_ge(*s_nt_ps.at(0, g + 1))
                dst = hT[:, g, :] if g < 12 else vcT[:, g - 12, :]
                fn(dst, bank(g % 4)[0:D2, :], ACT.Copy, scale=D2 ** -0.5 if g < 6 else 1.0).then_inc(s_nt_sb.sem, 1)
            fn(pj[:, :, O_GATE:O_GATE + 18], pj[:, :, O_GATE:O_GATE + 18], ACT.Sigmoid).then_inc(s_sm_act.sem, 1)
            for i in range(MT):
                last = fn(pj[:, i, O_Z:O_Z + 384], pj[:, i, O_Z:O_Z + 384], ACT.Silu)
            last.then_inc(s_sm_act.sem, 1)
            act.wait_ge(*s_sm_dve.at(0, 8))
            fn(ss[:, SQ:SQ + 24], ss[:, SQ:SQ + 24], ACT.Sqrt, scale=1.0 / D2, bias=eps[:, 0:1]).then_inc(s_sm_act.sem, 1)
            act.wait_ge(*s_hc_ps.at(0, 4))
            fn(hidc[:, :, :], bank(4)[0:D2, :].rearrange("p (s n) -> p s n", s=2), ACT.Silu).then_inc(s_hc_sb.sem, 1)
            act.wait_ge(*s_sm_dve.at(0, 10))
            fn(ss[0:32, SY:SY + 2], ss[0:32, SY:SY + 2], ACT.Sqrt, scale=1.0 / D2, bias=eps[0:32, 0:1]).then_inc(s_sm_act.sem, 1)
            for i in range(MT):
                act.wait_ge(*s_cs_mx.at(0, i + 1))
                fn(csc, csc, ACT.Exp).then_inc(s_cs_e.sem, 1)
                act.wait_ge(*s_ct_ps.at(0, i + 1))
                fn(pcT[:, :, :], bank(4, 768)[0:32, :].rearrange("p (h n) -> p h n", h=6)).then_inc(s_ct_sb.sem, 1)

            def exps(u):
                i, br, h = nsa[u]
                act.wait_ge(*s_ns_mx.at(0, u + 1))
                if u >= 3:
                    act.wait_ge(*s_nt2_ps.at(0, u - 2))
                at = SQ + (h if (u // 6) % 2 == 0 else 6 + h)
                fn(nprobs[u % 3][:, 0:(i + 1) * P], bank(u % 2, (i + 1) * P), ACT.Exp,
                       bias=red[:, u % 2:u % 2 + 1], accum_out=ss[:, at:at + 1]).then_inc(s_ns_e.sem, 1)

            exps(0)
            for u in range(NUNITS):
                if u + 1 < NUNITS:
                    if (u + 1) % 6 == 0 and u + 1 >= 12:
                        act.wait_ge(*s_o_acc.at(0, 4 + (u + 1) // 6 - 1))
                    exps(u + 1)
                i, br, h = nsa[u]
                act.wait_ge(*s_nt2_ps.at(0, u + 1))
                fn(npt[u % 2][:, 0:i + 1, :], bank(2 + u % 2, (i + 1) * P).rearrange("p (k n) -> p k n", n=P)).then_inc(s_nt2_sb.sem, 1)
            for g in range(4):
                act.wait_ge(*s_mt_ps.at(0, g + 1))
                fn(mT[:, g, :], bank(g)[0:D2, :]).then_inc(s_mt_sb.sem, 1)
            for k in range(2):
                act.wait_ge(*s_yc_ps.at(0, k + 1))
                fn(ycm[:, 6 + k, :], bank(4 + k), ACT.Copy, scale=vflat[:, 36 + k:37 + k]).then_inc(s_y_cm.sem, 1)
            for k in range(6):
                act.wait_ge(*s_yt_ps.at(0, k + 1))
                fn(ycm[:, k, :], bank(k % 4)).then_inc(s_y_cm.sem, 1)
            norm_sums(5, rc[:, RD:RD + DM])
            norm_drain(5, 1)
            for f in range(2):
                with act.Fori(0, 2) as turn:
                    for g in range(8):
                        act.wait_ge(*s_hid_ps.at(2, 16 * f + 8 * turn + g + 1))
                        fn(hid[:, 8 * turn + g, 0:TOK], bank(2 * (g % 2)), ACT.Relu).then_inc(s_hid_relu.sem, 1)

        def second_pe(pe, take, turn, norm, product, token_major):
            M = ((0, TOK),)
            pe.wait_ge(*s_par2.at(0, 16 * 14))
            pe.wait_ge(*s_ff_added.at(DEPTH - 1, 2 * MT))
            for c in range(9):
                turn(bank(5, CTAPS, CTAPS * c), rb[0:CTAPS, c * P:(c + 1) * P])
            for j in range(KT):
                turn(bank(5, 2, 36 + 2 * j), rb[0:2, QKV + j * P:QKV + (j + 1) * P])
            for j in range(2):
                turn(bank(5, 1, 52 + j), rb[0:1, 2176 + j * P:2176 + (j + 1) * P])
            turn(bank(6, 64)[0:D2, :], rb[0:64, 2432:2496]).then_inc(s_col2_ps.sem, 1)
            norm(4, gv_tm, ())
            pe.wait_ge(*s_norm_ht.at(4, KT))
            pe.wait_ge(*s_col2_sb.at(0, 1))
            for c in range(9):
                if c % 3 == 0:
                    slot = take()
                if c >= 2:
                    pe.wait_ge(*s_cv_sb.at(0, c - 1))
                product(2 * (c % 2), slot, c % 3, ht, M).then_inc(s_cv_ps.sem, 1)
            for b in range(4):
                token_major(s_pj_ps, 0, s_pj_sb, 4 * b, MT, ht, (), width=min(COLS, PJW - b * COLS))
            for c in range(9):
                pe.wait_ge(*s_cv_act.at(0, c + 1))
                if c < 4:
                    pe.wait_ge(*s_pj_sb.at(0, 16))
                else:
                    pe.wait_ge(*s_tm_sb.at(0, c - 3))
                for i in range(MT):
                    last = turn(bank(4 + c % 4, P, i * P), conv_out[:, c, i * P:(i + 1) * P])
                last.then_inc(s_tm_ps.sem, 1)
            pe.wait_ge(*s_sm_dve.at(0, 3))
            pe.wait_ge(*s_cv_sb.at(0, 9))
            for k, m in enumerate(("prefix", "same", "first", "last")):
                last = pe.matmul(bank(0, 24, 24 * k), mask[m], small[:, G, :], start=True, stop=True)
            last.then_inc(s_gs_ps.sem, 1)

            def heads_cm(g):
                if g >= 4:
                    pe.wait_ge(*s_h2_sb.at(0, g - 3))
                at = (0, 384, 0)[g // 6] + (g % 6) * D2
                for i in range(MT):
                    last = turn(bank(g % 4, P, i * P)[0:D2, :], qkv2[:, i, at:at + D2])
                last.then_inc(s_h2_ps.sem, 1)

            pe.wait_ge(*s_qk2.at(0, 1))
            for g in range(12):
                heads_cm(g)
            pe.wait_ge(*s_h2_sb.at(0, 12))
            pe.wait_ge(*s_tm_sb.at(0, 9))
            for u in range(8):
                i, h0, b0 = u // 2, 3 * (u % 2), 4 * (u % 2)
                if u >= 2:
                    pe.wait_ge(*s_lq.at(0, u - 1))
                for h in range(3):
                    at = 6 * i + h0 + h
                    gb = small[:, G, at:at + 1].to_broadcast([P, P])
                    for b, m in ((0, "far"), (1, "near")):
                        pe.matmul(bank(b0 + b, P, h * P), gb, mask["prefix"], start=True, stop=False)
                        pe.matmul(bank(b0 + b, P, h * P), ident[:, :], mask[m], start=False, stop=True)
                    k_ = kT[:, h0 + h, i * P:(i + 1) * P]
                    pe.matmul(bank(b0 + 2, P, h * P), k_, k_, start=True, stop=True)
                    last = pe.matmul(bank(b0 + 3, P, h * P), k_, qT[:, h0 + h, i * P:(i + 1) * P],
                                     start=True, stop=True)
                last.then_inc(s_dec_ps.sem, 1)
            pe.wait_ge(*s_lq.at(0, 8))
            for u in range(8):
                for h in range(3):
                    last = turn(bank(u, P, h * P), lm[:, u, h, :])
                last.then_inc(s_lt_ps.sem, 1)
            pe.wait_ge(*s_qd2.at(0, 1))
            pe.wait_ge(*s_x0.at(0, 8))
            pe.wait_ge(*s_lt_sb.at(0, 8))
            for g in range(12, 18):
                heads_cm(g)
            pe.wait_ge(*s_h2_sb.at(0, 18))
            with pe.Fori(0, 5) as level:
                def first(u):
                    pe.wait_ge(*s_bt.at(0, 8 * level + u + 1))
                    if u >= 2:
                        pe.wait_ge(*s_p1_sb.at(0, 8 * level + u - 1))
                    for h in range(3):
                        last = pe.matmul(bank(u % 2, P, h * P), bt[:, u % 4, h, :], xi[:, u, h, :],
                                         start=True, stop=True)
                    last.then_inc(s_p1_ps.sem, 1)

                first(0)
                first(1)
                for u in range(8):
                    if u + 2 < 8:
                        first(u + 2)
                    pe.wait_ge(*s_p1_sb.at(0, 8 * level + u + 1))
                    if u >= 3:
                        pe.wait_ge(*s_xx_sb.at(0, 8 * level + u - 2))
                    for h in range(3):
                        pe.matmul(bank(2 + u % 3, P, h * P), xit[:, u, h, :], lm[:, u, h, :], start=True, stop=True)
                        last = pe.matmul(bank(5 + u % 3, P, h * P), lm[:, u, h, :], xit[:, u, h, :],
                                         start=True, stop=True)
                    last.then_inc(s_xx_ps.sem, 1)
                pe.wait_ge(*s_xx_sb.at(0, 8 * level + 8))
            pe.wait_ge(*s_xx_sb.at(0, 40))
            pe.wait_ge(*s_vb2.at(0, 1))
            for u in range(8):
                i, h0 = u // 2, 3 * (u % 2)
                if u >= 2:
                    pe.wait_ge(*s_w_sb.at(0, u - 1))
                    pe.wait_ge(*s_u_sb.at(0, u - 1))
                for h in range(3):
                    at = (h0 + h) * D2
                    pe.matmul(bank(2 * (u % 2), P, h * P)[0:D2, :], kbe[:, i, at:at + D2], xit[:, u, h, :],
                              start=True, stop=True)
                    last = pe.matmul(bank(2 * (u % 2) + 1, D2, h * D2), xit[:, u, h, :],
                                     qkv2[:, i, 768 + at:768 + at + D2], start=True, stop=True)
                last.then_inc(s_wu_ps.sem, 1)
            pe.wait_ge(*s_w_sb.at(0, 8))
            pe.wait_ge(*s_u_sb.at(0, 8))
            for c in range(NCH):
                i, r0 = c // 2, CH2 * (c % 2)
                r, col = slice(r0, r0 + CH2), slice(c * CH2, (c + 1) * CH2)
                pe.wait_ge(*s_s_up.at(0, c + 1))
                for h in range(H2):
                    last = pe.matmul(bank(0, D2, h * D2)[r, :], kT[:, h, col], state[:, h * D2:(h + 1) * D2],
                                     start=True, stop=True)
                last.then_inc(s_vs_ps.sem, 1)
                pe.wait_ge(*s_vn.at(0, c + 1))
                if c >= 2:
                    pe.wait_ge(*s_oi_sb.at(0, c - 1))
                for h in range(H2):
                    vn = qkv2[r, i, 768 + h * D2:768 + (h + 1) * D2]
                    pe.matmul(bank(3, D2, h * D2)[0:D2, :], kdec[r, i, h * D2:(h + 1) * D2], vn,
                              start=True, stop=True)
                    pe.matmul(bank(1 + c % 2, D2, h * D2)[r, :], qT[:, h, col], state[:, h * D2:(h + 1) * D2],
                              start=True, stop=True)
                    last = pe.matmul(bank(4 + c % 2, D2, h * D2)[r, :], qkt[r, 2 * i + h // 3, h % 3, r0:r0 + CH2], vn,
                                     start=True, stop=True)
                last.then_inc(s_o2_ps.sem, 1)
            pe.wait_ge(*s_sm_dve.at(0, 7))
            pe.wait_ge(*s_oi_sb.at(0, NCH))
            pe.wait_ge(*s_s_up.at(0, NCH + 1))
            src = ([O_Q + D2 * h for h in range(6)] + [O_KV + 256 + D2 * h for h in range(2)]
                   + [O_KV + 512 + D2 * h for h in range(2)] + [O_KV + D2 * h for h in range(2)]
                   + [O_KV + 128 + D2 * h for h in range(2)])
            for g in range(14):
                if g >= 4:
                    pe.wait_ge(*s_nt_sb.at(0, g - 3))
                for i in range(MT):
                    last = turn(bank(g % 4, P, i * P)[0:D2, :], pj[:, i, src[g]:src[g] + D2])
                last.then_inc(s_nt_ps.sem, 1)
            pe.wait_ge(*s_kp.at(0, 2))
            for s in range(2):
                for r in range(2):
                    slot = take()
                    w1 = ring[0:D2, slot, :, :].rearrange("p a b -> p (a b)").rearrange("p (t n) -> p t n", t=16)
                    for k in range(16):
                        last = pe.matmul(bank(4, 256, 256 * s)[0:D2, :], kp[:, s, 16 * r + k, :, :], w1[:, k, :],
                                         start=r == 0 and k == 0, stop=r == 1 and k == 15)
                    last.then_inc(s_hc_ps.sem, 1)
            pe.wait_ge(*s_hc_sb.at(0, 1))
            for s in range(2):
                for k in range(2):
                    last = turn(bank(5, D2, D2 * (2 * s + k)), hidc[:, s, k * P:(k + 1) * P])
            last.then_inc(s_hct_ps.sem, 1)
            pe.wait_ge(*s_hct_sb.at(0, 1))
            pe.wait_ge(*s_par3.at(0, 16 * 4))
            for s in range(2):
                for h in range(2):
                    for k in range(2):
                        last = pe.matmul(bank(6, D2, D2 * (2 * s + h))[0:32, :], hidT[:, s, k, 32 * h:32 * h + 32],
                                         w2c[:, s, k, :], start=k == 0, stop=k == 1)
            last.then_inc(s_ck_ps.sem, 1)
            pe.wait_ge(*s_sm_dve.at(0, 11))
            for h in range(2):
                last = turn(bank(7, 32, 32 * h)[0:D2, :], ck[:, h, :])
            last.then_inc(s_ckt_ps.sem, 1)
            pe.wait_ge(*s_ckt_sb.at(0, 1))
            pe.wait_ge(*s_nt_sb.at(0, 14))
            for i in range(MT):
                for h in range(NSAH):
                    last = pe.matmul(bank(i % 2, KEYS, KEYS * h), hT[:, h, i * P:(i + 1) * P], ckT[:, h // 3, :],
                                     start=True, stop=True)
                last.then_inc(s_cs_ps.sem, 1)
                pe.wait_ge(*s_cs_p.at(0, i + 1))
                for h in range(NSAH):
                    last = turn(bank(4, P, h * P)[0:32, :], csc[:, KEYS * h:KEYS * h + KEYS])
                last.then_inc(s_ct_ps.sem, 1)
                pe.wait_ge(*s_ct_sb.at(0, i + 1))
                if i:
                    pe.wait_ge(*s_o_acc.at(0, i))
                for h in range(NSAH):
                    last = pe.matmul(bank(6, D2, h * D2), pcT[:, h, :], ck[:, 2 + h // 3, :], start=True, stop=True)
                last.then_inc(s_co_ps.sem, 1)

            def scores(u):
                i, br, h = nsa[u]
                n = (i + 1) * P
                if u >= 2:
                    pe.wait_ge(*s_ns_e.at(0, u - 1))
                pe.matmul(bank(u % 2, n), hT[:, h, i * P:(i + 1) * P], hT[:, 4 + 2 * br + h // 3, 0:n],
                          start=True, stop=False)
                pe.matmul(bank(u % 2, P, i * P), ident[:, :], rows2[:, R_CM:R_CM + P], start=False, stop=True).then_inc(s_ns_ps.sem, 1)

            pe.wait_ge(*s_o_acc.at(0, 4))
            def output(u):
                i, br, h = nsa[u]
                pe.wait_ge(*s_nt2_sb.at(0, u + 1))
                run = u // 6
                if h == 0 and run >= 2:
                    pe.wait_ge(*s_o_acc.at(0, 4 + run - 1))
                for k in range(i + 1):
                    v = VOFF[br] + (h // 3) * D2
                    last = pe.matmul(bank(6 + run % 2, D2, h * D2), npt[u % 2][:, k, :], pj[:, k, v:v + D2],
                                     start=k == 0, stop=k == i)
                if h == NSAH - 1:
                    last.then_inc(s_no_ps.sem, 1)

            scores(0)
            scores(1)
            for u in range(NUNITS):
                if u + 2 < NUNITS:
                    scores(u + 2)
                pe.wait_ge(*s_ns_e.at(0, u + 1))
                if u >= 2:
                    pe.wait_ge(*s_nt2_sb.at(0, u - 1))
                for k in range(nsa[u][0] + 1):
                    last = turn(bank(2 + u % 2, P, k * P), nprobs[u % 3][:, k * P:(k + 1) * P])
                last.then_inc(s_nt2_ps.sem, 1)
                if u:
                    output(u - 1)
            output(NUNITS - 1)
            pe.wait_ge(*s_par3.at(0, 16 * 4))
            pe.wait_ge(*s_nt2_sb.at(0, NUNITS))
            for g in range(4):
                for i in range(MT):
                    u_ = [pj[:, k, O_U + g * D2:O_U + (g + 1) * D2] for k in range(MT)]
                    o = bank(g, P, i * P)[0:D2, :]
                    last = pe.matmul(o, u_[i], bands[:, 3 * g + (0 if i == 0 else 1), :], start=True, stop=i == 0)
                    if i:
                        last = pe.matmul(o, u_[i - 1], bands[:, 3 * g + 2, :], start=False, stop=True)
                last.then_inc(s_mt_ps.sem, 1)
            pe.wait_ge(*s_mt_sb.at(0, 4))
            for g in range(4):
                r = slice(D2 * (g % 2), D2 * (g % 2) + D2)
                last = pe.matmul(bank(4 + g // 2)[r, :], pw[:, g, :], mT[:, g, :], start=True, stop=True)
                if g % 2:
                    last.then_inc(s_yc_ps.sem, 1)
            pe.wait_ge(*s_o_acc.at(0, 12))
            for k in range(6):
                if k >= 4:
                    pe.wait_ge(*s_y_cm.at(0, 2 + k - 3))
                for i in range(MT):
                    s_ = pj[:, i, k * P:(k + 1) * P] if k < 3 else oacc[:, i, (k - 3) * P:(k - 2) * P]
                    last = turn(bank(k % 4, P, i * P), s_)
                last.then_inc(s_yt_ps.sem, 1)
            pe.wait_ge(*s_y_cm.at(0, 8))
            for c in range(2):
                token_major(s_xw_ps, 0, s_x_mid_part, 4 * c, MT, ycm, ())
            norm(5, xn_b, ())
            pe.wait_ge(*s_norm_ht.at(5, KT))
            for f in range(2):
                n0 = take.blocks
                with pe.Fori(0, 2) as turn_:
                    for g in range(8):
                        if g % 4 == 0:
                            take.blocks = n0 + g // 4
                            slot = take(turn_)
                        if g >= 2:
                            pe.wait_ge(*s_hid_relu.at(2, 16 * f + 8 * turn_ + g - 1))
                        product(2 * (g % 2), slot, g % 4, ht, M).then_inc(s_hid_ps.sem, 1)
                    pe.wait_ge(*s_hid_relu.at(2, 16 * f + 8 * turn_ + 8))
                take.blocks = n0 + 4
                pe.wait_ge(*s_hid_ready.at(2, 16 * f + 16))
                for c in range(2):
                    for kb in range(2):
                        slot = take()
                        for i in range(MT):
                            if kb == 0 and f + c:
                                pe.wait_ge(*s_ff_added.at(2, (2 * f + c - 1) * MT + i + 1))
                            for k in range(KT):
                                last = pe.matmul(bank(4 + i), hid[:, KT * kb + k, i * P:(i + 1) * P],
                                                 ring[:, slot, k, :], start=kb == 0 and k == 0,
                                                 stop=kb == 1 and k == KT - 1)
                            if kb or i == MT - 1:
                                last.then_inc(s_ff_ps.sem, 1)

        def second_dve(dve, ch, norm_rows):
            tt, ts, stt = dve.tensor_tensor, dve.tensor_scalar, dve.scalar_tensor_tensor

            def sm(r):
                return small[:, r, :]

            def th(ap):
                return ap.rearrange("p (t h) -> p t h", t=MT)

            def copy(dst, src_):
                return dve.tensor_copy(dst, src_)

            dve.wait_ge(*s_col2_ps.at(0, 1))
            ch.note(dve.memset(modc[:, :, :, :], 0.0))
            ch.note(copy(vflat[:, 0:36], bank(5, 36)))
            for p in range(2):
                ch.note(copy(fused[:, p, :, 0], bank(5, 16, 36).rearrange("p (k r) -> p k r", r=2)[:, :, p]))
            ch.note(copy(vflat[:, 36:38], bank(5, 2, 52)))
            copy(vflat[0:D2, 64:128], bank(6, 64)[0:D2, :]).then_inc(s_col2_sb.sem, 1)
            norm_rows(4, gv_tm)
            dve.wait_ge(*s_norm_ps.at(4, KT))
            dve.wait_ge(*s_col2_sb.at(0, 1))
            ch.link(dve.memset(conv_in[:, :, 0:CTAPS - 1], 0.0))
            for c in range(9):
                dve.wait_ge(*s_cv_sb.at(0, c + 1))
                w_ = lambda k: vflat[:, CTAPS * c + k:CTAPS * c + k + 1]
                ch.link(ts(conv_out[:, c, :], conv_in[:, c, 0:TOK], w_(0), None, ALU.mult))
                for k in range(1, CTAPS):
                    step = stt(conv_out[:, c, :], conv_in[:, c, k:k + TOK], w_(k), conv_out[:, c, :],
                               op0=ALU.mult, op1=ALU.add)
                    ch.link(step) if k < CTAPS - 1 else step.then_inc(s_cv_done.sem, 1)
            dve.wait_ge(*s_pj_sb.at(0, 16))
            dve.wait_ge(*s_par2.at(0, 16 * 14))
            ch.link(tt(th(sm(XA)), pj[:, :, O_A:O_A + 6], rep(rows2[:, R_DT:R_DT + 6], MT), ALU.add))
            stt(sm(AB), sm(XA), -1.0, sm(XA), op0=ALU.mult, op1=ALU.max).then_inc(s_sm_dve.sem, 1)
            dve.wait_ge(*s_sm_act.at(0, 1))
            ts(sm(UU), sm(EY), 1.0, None, ALU.add).then_inc(s_sm_dve.sem, 1)
            dve.wait_ge(*s_sm_act.at(0, 4))
            dve.wait_ge(*s_sm_dve.at(0, 2))
            ch.note(stt(sm(EY), sm(UU), 1.0, sm(EY), op0=ALU.subtract, op1=ALU.subtract))
            ch.link(dve.reciprocal(sm(KD), sm(UU)))
            ch.link(tt(sm(EY), sm(EY), sm(KD), ALU.mult))
            ch.link(tt(sm(LN_), sm(LN_), sm(EY), ALU.subtract))
            ch.link(stt(sm(LN_), sm(XA), 0.0, sm(LN_), op0=ALU.max, op1=ALU.add))
            ch.link(tt(th(sm(G)), th(sm(LN_)), rep(rows2[:, R_AL:R_AL + 6], MT), ALU.mult))
            ts(sm(G), sm(G), -1.0, None, ALU.mult).then_inc(s_sm_dve.sem, 1)
            dve.wait_ge(*s_gs_ps.at(0, 1))
            ch.note(copy(sm(GC), bank(0, 24)))
            ch.note(ts(sm(NGC), bank(0, 24), -1.0, None, ALU.mult))
            ch.link(copy(glast[:, :, :], bank(0, 48, 48).rearrange("p (a n) -> p a n", a=2)))
            tt(sm(KD), bank(0, 24, 24), sm(GC), ALU.subtract).then_inc(s_sm_dve.sem, 1)
            dve.wait_ge(*s_tm_sb.at(0, 9))
            for i in range(MT):
                sq = ra[:, 768 * i:768 * (i + 1)]
                ch.link(tt(sq, qkv2[:, i, 0:768], qkv2[:, i, 0:768], ALU.mult))
                last = dve.tensor_reduce(ss[:, SQ + 12 * i:SQ + 12 * i + 12], by_head(sq), AX.X, ALU.add)
                ch.note(last) if i < MT - 1 else last.then_inc(s_sm_dve.sem, 1)
            dve.wait_ge(*s_sm_act.at(0, 6))
            ch.link(dve.reciprocal(rstd[:, SQ:SQ + 48], ss[:, SQ:SQ + 48]))
            for i in range(MT):
                q_ = rstd[:, SQ + 12 * i:SQ + 12 * i + 6]
                ch.link(ts(q_, q_, D2 ** -0.5, None, ALU.mult))
                last = tt(by_head(qkv2[:, i, 0:768]), by_head(qkv2[:, i, 0:768]),
                          bc(rstd[:, SQ + 12 * i:SQ + 12 * i + 12], D2), ALU.mult)
                ch.link(last) if i < MT - 1 else last.then_inc(s_qk2.sem, 1)
            dve.wait_ge(*s_qk2.at(0, 1))
            for i in range(MT):
                a = slice(6 * i, 6 * i + 6)
                ch.link(tt(by_head(kbe[:, i, :]), by_head(qkv2[:, i, 384:768]), bc(small[:, BETA, a], D2), ALU.mult))
                ch.link(tt(by_head(kbe[:, i, :]), by_head(kbe[:, i, :]), bc(small[:, EGC, a], D2), ALU.mult))
                last = tt(by_head(qkv2[:, i, 768:1152]), by_head(qkv2[:, i, 768:1152]), bc(small[:, BETA, a], D2),
                          ALU.mult)
                ch.note(last) if i < MT - 1 else last.then_inc(s_vb2.sem, 1)
            for u in range(8):
                i, h0 = u // 2, 3 * (u % 2)
                dve.wait_ge(*s_dec_sb.at(0, u + 1))
                for h in range(3):
                    at = 6 * i + h0 + h
                    ch.note(stt(lm[:, u, h, :], bank(4 * (u % 2) + 2, P, h * P), small[:, BETA, at:at + 1],
                                lm[:, u, h, :], op0=ALU.mult, op1=ALU.mult))
                three = bank(4 * (u % 2) + 3, 384).rearrange("p (h n) -> p h n", h=3)
                tt(qkt[:, u, :, :], three, qkt[:, u, :, :], ALU.mult).then_inc(s_lq.sem, 1)
            dve.wait_ge(*s_h2_ps.at(0, 12))
            for i in range(MT):
                q_ = by_head(qkv2[:, i, 0:384])
                last = tt(q_, q_, bc(small[:, EGC, 6 * i:6 * i + 6], D2), ALU.mult)
            last.then_inc(s_qd2.sem, 1)
            dve.wait_ge(*s_lq.at(0, 8))
            for u in range(8):
                dve.wait_ge(*s_lt_sb.at(0, u + 1))
                ch.note(tt(xit[:, u, :, :], lt[:, u, :, :], rep(mask["pair_t"], 3), ALU.mult))
                ch.link(tt(xi[:, u, :, :], lm[:, u, :, :], rep(mask["pair"], 3), ALU.mult))
                ch.note(tt(xit[:, u, :, :], rep(ident[:, :], 3), xit[:, u, :, :], ALU.subtract))
                tt(xi[:, u, :, :], rep(ident[:, :], 3), xi[:, u, :, :], ALU.subtract).then_inc(s_x0.sem, 1)
            dve.wait_ge(*s_x0.at(0, 8))
            dve.wait_ge(*s_lt_sb.at(0, 8))
            with dve.Fori(0, 5) as level:
                def part(u):
                    if u >= 4:
                        dve.wait_ge(*s_p1_ps.at(0, 8 * level + u - 3))
                    tt(bt[:, u % 4, :, :], lt[:, u, :, :],
                           levels[:, level, :].unsqueeze(1).to_broadcast([P, 3, P]), ALU.mult).then_inc(s_bt.sem, 1)

                for u in range(4):
                    part(u)
                for u in range(8):
                    if u + 4 < 8:
                        part(u + 4)
                    dve.wait_ge(*s_xx_ps.at(0, 8 * level + u + 1))
                    ch_x = tt(xi[:, u, :, :], xi[:, u, :, :], bank(2 + u % 3, 384).rearrange("p (h n) -> p h n", h=3),
                              ALU.subtract)
                    tt(xit[:, u, :, :], xit[:, u, :, :], bank(5 + u % 3, 384).rearrange("p (h n) -> p h n", h=3),
                           ALU.subtract).then_inc(s_xx_sb.sem, 1)
                dve.wait_ge(*s_xx_sb.at(0, 8 * level + 8))
            dve.wait_ge(*s_p1_ps.at(0, 40))
            for i in range(MT):
                last = tt(by_head(kdec[:, i, :]), by_head(qkv2[:, i, 384:768]), bc(small[:, EKD, 6 * i:6 * i + 6], D2),
                          ALU.mult)
            ch.link(last)
            for u in range(8):
                i, h0 = u // 2, 3 * (u % 2)
                dve.wait_ge(*s_wu_ps.at(0, u + 1))
                copy(qkv2[:, i, 768 + h0 * D2:768 + (h0 + 3) * D2], bank(2 * (u % 2) + 1, 192)).then_inc(s_u_sb.sem, 1)
            dve.wait_ge(*s_u_sb.at(0, 8))
            dve.memset(state[:, :], 0.0).then_inc(s_s_up.sem, 1)
            for c in range(NCH):
                i, r0 = c // 2, CH2 * (c % 2)
                r = slice(r0, r0 + CH2)
                dve.wait_ge(*s_vs_ps.at(0, c + 1))
                v_ = qkv2[r, i, 768:1152]
                tt(v_, v_, bank(0, 384)[r, :], ALU.subtract).then_inc(s_vn.sem, 1)
                dve.wait_ge(*s_o2_ps.at(0, c + 1))
                dve.wait_ge(*s_s_up.at(0, c + 1))
                ch.link(tt(by_head(state[:, :]), by_head(state[:, :]),
                           bc(glast[0:D2, c % 2, 6 * i:6 * i + 6], D2), ALU.mult))
                tt(state[:, :], state[:, :], bank(3, 384)[0:D2, :], ALU.add).then_inc(s_s_up.sem, 1)
                dve.wait_ge(*s_o2_sb.at(0, c + 1))
                tt(qkv2[r, i, 0:384], qkv2[r, i, 0:384], bank(4 + c % 2, 384)[r, :], ALU.add).then_inc(s_oi_sb.sem, 1)
            groups = [(O_Q, 6, R_QN), (O_KV + 256, 2, R_KN + D2), (O_KV + 512, 2, R_KN + 2 * D2)]
            for i in range(MT):
                at = SQ + 10 * i
                for off, h, _ in groups:
                    sq = ra[:, 640 * i + D2 * (at - SQ - 10 * i):640 * i + D2 * (at - SQ - 10 * i + h)]
                    s_ = pj[:, i, off:off + h * D2]
                    ch.link(tt(sq, s_, s_, ALU.mult))
                    last = dve.tensor_reduce(ss[:, at:at + h], by_head(sq), AX.X, ALU.add)
                    at += h
                    ch.note(last) if at < SQ + 40 else last.then_inc(s_sm_dve.sem, 1)
            dve.wait_ge(*s_sm_act.at(0, 7))
            ch.link(dve.reciprocal(rstd[:, SQ:SQ + 40], ss[:, SQ:SQ + 40]))
            for i in range(MT):
                at = SQ + 10 * i
                for off, h, gain in groups:
                    s_ = by_head(pj[:, i, off:off + h * D2])
                    ch.link(tt(s_, s_, bc(rstd[:, at:at + h], D2), ALU.mult))
                    last = tt(s_, s_, rep(rows2[:, gain:gain + D2], h), ALU.mult)
                    at += h
                    ch.note(last) if at < SQ + 40 else last.then_inc(s_sm_dve.sem, 1)
            ch.link(dve.memset(ra[0:D2, 0:4096].rearrange("p (r n) -> p r n", n=KEYS)[:, :, KEYS - 1:KEYS], 0.0))
            for s in range(2):
                dve.wait_ge(*s_nt_sb.at(0, 12 + 2 * s))
                for h in range(2):
                    z = (hT[:, 10 + h, :] if s == 0 else vcT[:, h, :]).rearrange("p (r b) -> p b r", b=16)
                    for a in range(2):
                        last = tt(kp[:, s, 16 * a:16 * a + 16, h, 0:KEYS - 1], z[:, :, a:a + KEYS - 1],
                                  bc(vflat[0:D2, 64 + 32 * s + 16 * a:64 + 32 * s + 16 * a + 16], KEYS - 1), ALU.add)
                last.then_inc(s_kp.sem, 1)
            dve.wait_ge(*s_oi_sb.at(0, NCH))
            for i in range(MT):
                sq = qkv2[:, i, 384:768]
                ch.link(tt(sq, qkv2[:, i, 0:384], qkv2[:, i, 0:384], ALU.mult))
                last = dve.tensor_reduce(ss[:, SQ + 6 * i:SQ + 6 * i + 6], by_head(sq), AX.X, ALU.add)
                ch.note(last) if i < MT - 1 else last.then_inc(s_sm_dve.sem, 1)
            dve.wait_ge(*s_sm_act.at(0, 10))
            ch.link(dve.reciprocal(rstd[:, SQ:SQ + 24], ss[:, SQ:SQ + 24]))
            for i in range(MT):
                o_ = by_head(qkv2[:, i, 0:384])
                ch.link(tt(o_, o_, bc(rstd[:, SQ + 6 * i:SQ + 6 * i + 6], D2), ALU.mult))
                ch.link(tt(o_, o_, rep(rows2[:, R_GN:R_GN + D2], 6), ALU.mult))
                last = tt(pj[:, i, O_Z:O_Z + 384], pj[:, i, O_Z:O_Z + 384], qkv2[:, i, 0:384], ALU.mult)
                ch.note(last) if i < MT - 1 else last.then_inc(s_sm_dve.sem, 1)
            dve.wait_ge(*s_hct_ps.at(0, 1))
            copy(hidT[:, :, :, :], bank(5, 256).rearrange("p (s k n) -> p s k n", s=2, k=2)).then_inc(s_hct_sb.sem, 1)
            dve.wait_ge(*s_ck_ps.at(0, 1))
            ch.link(copy(ck[:, :, :], bank(6, 256)[0:32, :].rearrange("p (j d) -> p j d", j=4)))
            ch.link(tt(ctmp[0:32, 0:128].rearrange("p (j d) -> p j d", j=2), ck[:, 0:2, :], ck[:, 0:2, :], ALU.mult))
            dve.tensor_reduce(ss[0:32, SY:SY + 2], by_head(ctmp[0:32, 0:128]), AX.X, ALU.add).then_inc(s_sm_dve.sem, 1)
            dve.wait_ge(*s_sm_act.at(0, 11))
            ch.link(dve.reciprocal(rstd[0:32, SY:SY + 2], ss[0:32, SY:SY + 2]))
            ch.link(tt(ck[:, 0:2, :], ck[:, 0:2, :], bc(rstd[0:32, SY:SY + 2], D2), ALU.mult))
            tt(ck[:, 0:2, :], ck[:, 0:2, :], rep(rows2[0:32, R_KN:R_KN + D2], 2), ALU.mult).then_inc(s_sm_dve.sem, 1)
            dve.wait_ge(*s_ckt_ps.at(0, 1))
            copy(ckT[:, :, :], bank(7, 64)[0:D2, :].rearrange("p (h n) -> p h n", h=2)).then_inc(s_ckt_sb.sem, 1)

            def coefficient(i, br, at):
                ch.link(dve.reciprocal(rstd[:, at:at + 6], ss[:, at:at + 6]))
                gates = pj[:, i, O_GATE:O_GATE + 18].rearrange("p (h b) -> p h b", b=3)[:, :, br]
                ch.link(tt(rstd[:, at:at + 6], rstd[:, at:at + 6], gates, ALU.mult))

            for i in range(MT):
                sc = csc.rearrange("p (h n) -> p h n", n=KEYS)
                dve.wait_ge(*s_cs_ps.at(0, i + 1))
                if i:
                    dve.wait_ge(*s_ct_ps.at(0, i))
                ch.link(tt(sc, bank(i % 2, 192).rearrange("p (h n) -> p h n", n=KEYS), rep(cneg[:, i, :], 6), ALU.add))
                ch.link(dve.tensor_reduce(rstd[:, SY:SY + 6], sc, AX.X, ALU.max))
                tt(sc, sc, bc(rstd[:, SY:SY + 6], KEYS), ALU.subtract).then_inc(s_cs_mx.sem, 1)
                dve.wait_ge(*s_cs_e.at(0, i + 1))
                ch.link(dve.tensor_reduce(ss[:, SN:SN + 6], sc, AX.X, ALU.add))
                tt(sc, sc, rep(cmask[:, i, :], 6), ALU.mult).then_inc(s_cs_p.sem, 1)
                coefficient(i, 0, SN)
                dve.wait_ge(*s_co_ps.at(0, i + 1))
                tt(by_head(oacc[:, i, :]), by_head(bank(6, 384)), bc(rstd[:, SN:SN + 6], D2), ALU.mult).then_inc(s_o_acc.sem, 1)

            def peak(u):
                i, br, h = nsa[u]
                dve.wait_ge(*s_ns_ps.at(0, u + 1))
                ch.link(dve.tensor_reduce(red[:, 6 + u % 2:7 + u % 2], bank(u % 2, (i + 1) * P), AX.X, ALU.max))
                ts(red[:, u % 2:u % 2 + 1], red[:, 6 + u % 2:7 + u % 2], -1.0, None, ALU.mult).then_inc(s_ns_mx.sem, 1)

            for u in range(NUNITS):
                i, br, h = nsa[u]
                if u >= 2:
                    dve.wait_ge(*s_ns_e.at(0, u - 1))
                peak(u)
                if u >= 8 and (u - 8) % 6 == 0 or u == NUNITS - 1:
                    for run in ([(u - 8) // 6] if u < NUNITS - 1 else [7]):
                        fold(dve, ch, run, coefficient)
            for c in range(2):
                for i in range(MT):
                    dve.wait_ge(*s_xw_ps.at(0, 4 * c + i + 1))
                    xs = x[:, i, c * COLS:(c + 1) * COLS]
                    tt(xs, xs, bank(4 + i), ALU.add).then_inc(s_x_mid_part.sem, 1)
            dve.wait_ge(*s_x_mid_part.at(0, 8))
            norm_rows(5, xn_b)
            for f in range(2):
                with dve.Fori(0, 2) as turn:
                    for g in range(8):
                        dve.wait_ge(*s_hid_relu.at(2, 16 * f + 8 * turn + g + 1))
                        h_ = hid[:, 8 * turn + g, 0:TOK]
                        tt(h_, h_, h_, ALU.mult).then_inc(s_hid_ready.sem, 1)
                for c in range(2):
                    for i in range(MT):
                        dve.wait_ge(*s_ff_ps.at(2, (2 * f + c) * 5 + 2 + i))
                        xs = x[:, i, c * COLS:(c + 1) * COLS]
                        tt(xs, xs, bank(4 + i), ALU.add).then_inc(s_ff_added.sem, 1)

        def fold(dve, ch, run, coefficient):
            i, br = run // 2, 1 + run % 2
            dve.wait_ge(*s_no_ps.at(0, run + 1))
            dve.wait_ge(*s_ns_e.at(0, 6 * run + 6))
            at = SQ + 6 * (run % 2)
            coefficient(i, br, at)
            ch.link(dve.tensor_tensor(by_head(otmp), by_head(bank(6 + run % 2, 384)), bc(rstd[:, at:at + 6], D2),
                                      ALU.mult))
            dve.tensor_tensor(oacc[:, i, :], oacc[:, i, :], otmp, ALU.add).then_inc(s_o_acc.sem, 1)

        s_qk2 = signal("qk2", 1)
        s_vb2 = signal("vb2", 1)
        s_qd2 = signal("qd2", 1)
        s_x_mid_part = signal("x_mid_part", 8)

        block = ctx.enter_context(nc.Block())

        @block.sync
        def _(sp):
            loaded = [0]

            def fetch(src, freed, width=COLS, rows=P):
                slot = loaded[0] % 2
                loaded[0] += 1
                if freed:
                    sp.wait_ge(*freed)
                dst = ring[0:rows, slot, :, 0:width]
                if rows == D2:
                    dst = ring[0:rows, slot, :, :].rearrange("p a b -> p (a b)").rearrange("p (t n) -> p t n", t=16)
                sp.dma_start(dst, src).then_inc(wl[slot], 16)

            def mlp(w1, w2, run, n, freed):
                up = 1 + n
                for f in range(2):
                    first = freed if f == 0 else (s_ff_ps.at(run, up + 1), s_ff_ps.at(run, 2 * up))
                    block1 = cols(w1, f * 2048)
                    fetch(block1(0), first[0])
                    fetch(block1(1), first[1])
                    for i in (2, 3):
                        fetch(block1(i), s_hid_ps.at(run, 16 * f + 4 * i - 4))
                    for c in range(2):
                        base = 2 * f * up
                        fetch(cols(w2, c * COLS, f * 2048)(0),
                              s_ff_ps.at(run, base + 1) if c else s_hid_ps.at(run, 16 * f + 12))
                        fetch(cols(w2, c * COLS, f * 2048 + DM)(0),
                              s_ff_ps.at(run, base + up) if c else s_hid_ps.at(run, 16 * f + 16))

            for l in range(DEPTH):
                n = NT[l]
                w = t["w_in"][l]
                ada = cols(t["ada_w"][l], 0)
                for i in range(2):
                    before = s_ff_ps.at(l - 1, 3 * (1 + NT[0]) + (1 + NT[0] if i else 1)) if l else None
                    fetch(ada(i), before)
                with sp.Fori(1, 6) as j:
                    for i in range(2):
                        fetch(ada(2 * j + i), s_ada_ps.at(l, 2 * j + i - 1))
                q, gu, gv = cols(w, 0), cols(w, GU_OFF), cols(w, GV_OFF)
                cgb, cga = cols(w, CG_OFF + DM), cols(w, CG_OFF)
                fetch(q(0), s_ada_ps.at(l, 11))
                fetch(q(1), s_ada_ps.at(l, 12))
                fetch(q(2), s_qkv_ps.at(l, n))
                fetch(gu(0), s_qkv_ps.at(l, 2 * n))
                fetch(gu(1), s_qkv_ps.at(l, 2 * n + AT))
                fetch(gv(0), s_gu_ps.at(l, 4))
                fetch(gv(1), s_gu_ps.at(l, 8))
                fetch(cgb(0), s_gv_ps.at(l, n))
                fetch(cgb(1), s_gv_ps.at(l, 2 * n))
                fetch(cga(0), s_cgb_ps.at(l, 4))
                fetch(cga(1), s_cgb_ps.at(l, 8))
                gate_free, out_free = s_cga_ps.at(l, 4), s_cga_ps.at(l, 8)
                for b, (gi, wo) in enumerate(((1, "w_gmlp_o"), (0, "w_attn_o"), (2, "w_conv_o"))):
                    for c in range(2):
                        fetch(cols(w, GATE_OFF + gi * DM)(c), gate_free)
                        fetch(cols(t[wo][l], 0)(c), out_free)
                        gate_free, out_free = s_bg_ps.at(3 * l + b, 4 * c + 4), s_bo_ps.at(3 * l + b, 4 * c + 4)
                fetch(cols(t["w_out"][l], 0)(0), gate_free)
                fetch(cols(t["w_out"][l], 0)(1), out_free)
                mlp(t["w_ff1"][l], t["w_ff2"][l], l, n, (s_y_ps.at(l, n), s_y_ps.at(l, 2 * n)))
            w = t["w_in_2"][0].rearrange("(t p) n -> p t n", p=P)
            last = 3 * (1 + MT)
            for i, freed in enumerate((s_ff_ps.at(DEPTH - 1, last + 1), s_ff_ps.at(DEPTH - 1, last + 1 + MT),
                                       s_cv_ps.at(0, 3))):
                fetch(w[:, :, i * 384:(i + 1) * 384], freed, 384)
            for i, freed in enumerate((s_cv_ps.at(0, 6), s_cv_ps.at(0, 9), s_pj_ps.at(0, 4), s_pj_ps.at(0, 8))):
                width = min(COLS, PJW - i * COLS)
                fetch(w[:, :, QKV + i * COLS:QKV + i * COLS + width], freed, width)
            for i, freed in enumerate((s_pj_ps.at(0, 12), s_pj_ps.at(0, 16), s_hc_ps.at(0, 1), s_hc_ps.at(0, 2))):
                rows = t["cmp_w1_2"][0, i // 2, (i % 2) * 1024:(i % 2 + 1) * 1024, :]
                fetch(rows.rearrange("(t d) n -> d t n", d=D2), freed, rows=D2)
            fetch(cols(t["w_out_2"][0], 0)(0), s_hc_ps.at(0, 3))
            fetch(cols(t["w_out_2"][0], 0)(1), s_hc_ps.at(0, 4))
            mlp(t["w_ffn1_2"][0], t["w_ffn2_2"][0], DEPTH, MT, (s_xw_ps.at(0, 4), s_xw_ps.at(0, 8)))
            sp.wait_ge(*s_ff_added.at(DEPTH, 4 * MT))
            sp.dma_start(out, x[:, 0:MT, :]).then_inc(s_out_stored.sem, 16)
            sp.wait_ge(*s_out_stored.at(0, 16))

        @block.gpsimd
        def _(pool):
            ch = Chain(pool, chain_sem["pool"])

            def load(dst, src, name):
                pool.dma_start(dst, src).then_inc(name.sem, 16)

            load(ident[:, :], t["ident"], s_const_in)
            load(rope[:, :, :], t["rope"].rearrange("(t p) d -> p t d", p=P), s_const_in)
            load(rb[0:1, 0:DM], t["c"], s_c_in)
            load(rb[1:2, 0:DM], t["c_ctx"].rearrange("(a n) -> a n", a=1), s_c_in)
            load(x[:, 0:MT, :], t["x"][0].rearrange("(t p) d -> p t d", p=P), s_x_in)
            load(x[:, MT:AT, :], t["ctx"][0].rearrange("(t p) d -> p t d", p=P), s_x_in)
            for l in range(DEPTH):
                n = NT[l]
                if l:
                    pool.wait_ge(*s_x_ready.at(2 * l - 1, 1))
                else:
                    pool.wait_ge(*s_c_ready.at(0, 1))
                for r in range(2):
                    load(rb[r:r + 1, :], t["ada_b"][l:l + 1, :], s_adab_in)
                load(rc[0:CONVK, 0:DM], t["conv_w"][l], s_vecs_in)
                for r, v in enumerate(("mix_pre_g", "gmlp_norm_g", "conv_b", "conv_norm_g", "conv_norm_b",
                                       "ffn_pre_g")):
                    load(rc[CONVK + r:CONVK + r + 1, 0:DM], t[v][l:l + 1, :], s_vecs_in)
                load(gains[:, 0, :], t["q_norm_g"][l:l + 1, :].to_broadcast([P, HD]), s_gain_in)
                load(gains[:, 1, :], t["k_norm_g"][l:l + 1, :].to_broadcast([P, HD]), s_gain_in)
                pool.wait_ge(*s_ada_row.at(l, 12))
                pool.dma_start(mods[l], ra[0:2, 0:6 * DM]).then_inc(s_mods_out.sem, 16)
                pool.wait_ge(*s_att_sb.at(l, OH[l]))
                load(ws_raw, t["gmlp_ws"][l].rearrange("g p q -> p g q"), s_ws_in)
                load(bs_row, t["gmlp_bs"][l:l + 1].to_broadcast([P, 4, P]), s_ws_in)
                pool.wait_ge(*s_sv_ps.at(l, KT))
                glu = rc[:, RD + GW:RD + (KT + 1) * GW].rearrange("p (k w) -> p k w", w=GW)
                pool.memset(glu[:, :, 0:PAD], 0.0)
                pool.memset(glu[:, :, PAD + TOK:2 * PAD + TOK + PAD], 0.0)
                pool.memset(glu[:, :, GW - PAD:GW], 0.0).then_inc(s_pads.sem, 1)
                for b in range(3):
                    run = 3 * l + b
                    for j in range(KT):
                        pool.wait_ge(*s_bo_sb.at(run, j + 1))
                        o = branch[:, j % 2, 0:n * P]
                        g = gate4[:, j % 4, 0:n * P]
                        if b == 0:
                            pool.tensor_tensor(acc[:, j, 0:n * P], o, g, ALU.mult).then_inc(s_merged.sem, 1)
                        else:
                            ch.link(pool.tensor_tensor(o, o, g, ALU.mult))
                            pool.tensor_tensor(acc[:, j, 0:n * P], acc[:, j, 0:n * P], o, ALU.add).then_inc(s_merged.sem, 1)
                pool.wait_ge(*s_bo_ps.at(3 * l + 2, KT))
                pool.wait_ge(*s_mods_out.at(l, 16))
                for k, (dst, part, gn) in enumerate(((rc, 2, "mix_post_g"), (rb, 5, "ffn_post_g"))):
                    if k:
                        pool.wait_ge(*s_norm_ps.at(2 * l + 1, KT))
                    for v in range(2):
                        load(dst[:, v * DM:(v + 1) * DM],
                             mods[l, v:v + 1, part * DM:(part + 1) * DM].to_broadcast([P, DM]), s_post_in)
                    load(dst[:, 2 * DM:3 * DM], t[gn][l:l + 1, :].to_broadcast([P, DM]), s_post_in)
            second_pool(pool, ch, load)

        def units(l):
            us = [(h, i * P, i, range(AT), i == MT - 1) for h in range(HEADS) for i in range(MT)]
            if NT[l] == AT:
                us += [(h, TOK + i * P, i, range(MT, AT), i == CT - 1) for h in range(HEADS) for i in range(CT)]
            return us

        def streams(l):
            return ((0, TOK), (TOK, CTX)) if NT[l] == AT else ((0, TOK),)

        @block.scalar
        def _(act):
            ch = Chain(act, chain_sem["act"])

            def fn(out_, in_, f=ACT.Copy, **kw):
                return act.activation(out_, in_, f, **kw)

            def root(at, n, width, name):
                fn(ss[:, at:at + n], ss[:, at:at + n], ACT.Sqrt, scale=1.0 / width, bias=eps[:, 0:1]).then_inc(name.sem, 1)

            def norm_sums(run, junk):
                n = NORM_T[run]
                for i in range(n):
                    if run == 2 * DEPTH + 1:
                        act.wait_ge(*s_x_mid_part.at(0, n + i + 1))
                    elif run and i < n - 1:
                        act.wait_ge(*s_x_added.at(run - 1, i + 1))
                    elif run:
                        act.wait_ge(*s_x_ready.at(run - 1, 1))
                    ch.link(fn(junk, x[:, i, :], ACT.Square, accum_out=ss[:, SN + i:SN + i + 1]))
                root(SN, n, DM, s_norm_rms)

            def norm_drain(run, part):
                for j in range(KT):
                    act.wait_ge(*s_norm_ps.at(run, j + 1))
                    for v, (a, m) in enumerate(((0, TOK), (TOK, CTX))):
                        if v and NORM_T[run] == MT:
                            continue
                        last = fn(ht[:, j, a:a + m], bank(2 * (j % 2) + v, m), ACT.Identity,
                                  scale=fused[:, part, j, v:v + 1], bias=modc[:, 2 * part, j, v:v + 1])
                    last.then_inc(s_norm_ht.sem, 1)

            def drain(name, l, out_name, out_of, base, f, streams_=None):
                for j in range(KT):
                    act.wait_ge(*name.at(l, j + 1))
                    for v, (a, m) in enumerate(streams_ or streams(l)):
                        last = fn(out_of(j, v, a, m), bank(base + 2 * (j % 2) + v, m), f)
                    last.then_inc(out_name.sem, 1)

            def attention(l):
                us = units(l)

                def exps(u):
                    nk = len(us[u][3])
                    act.wait_ge(*s_att_mx.at(l, u + 1))
                    if u >= 3:
                        act.wait_ge(*s_att_t.at(l, u - 2))
                    fn(probs[u % 3][:, 0:nk * P], bank(2 * (u % 2), nk * P), ACT.Exp,
                           scale=HD ** -0.5, bias=red[:, u % 2:u % 2 + 1],
                           accum_out=red[:, 2 + u % 2:3 + u % 2]).then_inc(s_att_e.sem, 1)

                heads = [u for u in range(len(us)) if us[u][4]]

                def head(o):
                    h, col = us[heads[o]][0:2]
                    a, m = (0, TOK) if col < TOK else (TOK, CTX)
                    act.wait_ge(*s_att_o.at(l, o + 1))
                    fn(q_cm[:, h, a:a + m], bank(6 + o % 2, m)).then_inc(s_att_sb.sem, 1)

                exps(0)
                for u in range(len(us)):
                    i, nk = us[u][2], len(us[u][3])
                    if u + 1 < len(us):
                        exps(u + 1)
                    if u - 1 in heads:
                        head(heads.index(u - 1))
                    act.wait_ge(*s_att_t.at(l, u + 1))
                    fn(PT[:, 0:nk, i * P:(i + 1) * P],
                           bank(4, nk * P).rearrange("p (k n) -> p k n", k=nk)).then_inc(s_att_pt.sem, 1)
                head(len(heads) - 1)

            def conv_norm(l):
                for j in range(KT):
                    act.wait_ge(*s_centred.at(l, j + 1))
                    for v, (a, m) in enumerate(streams(l)):
                        last = fn(u_cm[:, j, a:a + m], conv_slot(j, v * (TOK + 2 * PAD), m), ACT.Square)
                    last.then_inc(s_squared.sem, 1)
                act.wait_ge(*s_var_ps.at(l, 1))
                for v, (a, m) in enumerate(streams(l)):
                    last = fn(kt[:, 1, a:a + m], bank(6 + v, m), ACT.Sqrt, scale=1.0 / DM, bias=eps[:, 0:1])
                last.then_inc(s_std_sb.sem, 1)
                for j in range(KT):
                    act.wait_ge(*s_normed.at(l, j + 1))
                    for v, (a, m) in enumerate(streams(l)):
                        last = fn(u_cm[:, j, a:a + m], conv_slot(j, v * (TOK + 2 * PAD), m), ACT.Silu,
                                  scale=vec[:, j, CONVK + 3:CONVK + 4], bias=vec[:, j, CONVK + 4:CONVK + 5])
                    last.then_inc(s_conv_cm.sem, 1)

            act.wait_ge(*s_c_in.at(0, 32))
            fn(rb[0:2, 0:DM], rb[0:2, 0:DM], ACT.Silu).then_inc(s_c_silu.sem, 1)
            for l in range(DEPTH):
                n = NT[l]
                if l == 0:
                    act.wait_ge(*s_x_in.at(0, 32))
                    act.wait_ge(*s_consts.at(0, 1))
                norm_sums(2 * l, rc[:, 1024:2048])
                act.wait_ge(*s_cols_ready.at(l, 1))
                norm_drain(2 * l, 0)
                act.wait_ge(*s_mods_out.at(l, 16))
                g = 0
                for b in range(3):
                    for i in range(n if b < 2 else AT):
                        act.wait_ge(*s_qkv_ps.at(l, g + 1))
                        fn(q_tm[:, b, i, :] if b < 2 else kv[:, i, :], bank(4 + g % 4))
                        if g >= 8:
                            act.wait_ge(*s_qkv_red.at(l, g - 7))
                        fn(ra[:, 512 * (g % 8):512 * (g % 8) + 512], bank(4 + g % 4), ACT.Square).then_inc(s_qkv_sb.sem, 1)
                        g += 1
                act.wait_ge(*s_qkv_red.at(l, g))
                root(SQ, 4 * 2 * n + 2 * AT, HD, s_qkv_rms)
                drain(s_gu_ps, l, s_gu_sb, lambda j, v, a, m: u_cm[:, j, a:a + m], 0, ACT.Gelu_apprx_tanh)
                for g in range(2 * n):
                    c, i = divmod(g, n)
                    act.wait_ge(*s_gv_ps.at(l, g + 1))
                    fn(gv_tm[:, i, c * COLS:(c + 1) * COLS], bank(4 + g % 4), ACT.Gelu_apprx_tanh).then_inc(s_gv_sb.sem, 1)
                act.wait_ge(*s_gv_sb.at(l, 2 * n))
                for i in range(n):
                    ch.link(fn(rc[:, 2 * RD:2 * RD + DM], gv_tm[:, i, :], ACT.Square,
                               accum_out=ss[:, SG + i:SG + i + 1]))
                root(SG, n, DM, s_gv_rms)
                for h in range(HEADS + KVH):
                    act.wait_ge(*s_qk_ps.at(l, h + 1))
                    dst = q_cm[:, h, :] if h < HEADS else kt[:, h - HEADS, :]
                    for v, (a, m) in enumerate(streams(l) if h < HEADS else streams(0)):
                        last = fn(dst[:, a:a + m], bank(2 * (h % 2) + v, m))
                    last.then_inc(s_qk_cm.sem, 1)
                attention(l)
                act.wait_ge(*s_ws_ps.at(l, 1))
                fn(ws_t, bank(0).rearrange("p (g q) -> p g q", g=4)).then_inc(s_ws_ready.sem, 1)
                act.wait_ge(*s_pads.at(l, 1))
                drain(s_cgb_ps, l, s_cgb_sb, lambda j, v, a, m: conv_slot(j + 1, PAD + v * (TOK + 2 * PAD), m),
                      4, ACT.Sigmoid)
                for b in range(3):
                    run = 3 * l + b
                    for c in range(2):
                        for j in range(4 * c, 4 * c + 4):
                            act.wait_ge(*s_bg_ps.at(run, j + 1))
                            if c:
                                act.wait_ge(*s_merged.at(run, j - 3))
                            elif b:
                                act.wait_ge(*s_merged.at(run - 1, j + 5))
                            for v, (a, m) in enumerate(streams(l)):
                                last = fn(gate4[:, j % 4, a:a + m], bank(4 + 2 * (j % 2) + v, m), ACT.Sigmoid)
                            last.then_inc(s_bg_sb.sem, 1)
                        if b == 2 and c == 0:
                            conv_norm(l)
                        for j in range(4 * c, 4 * c + 4):
                            act.wait_ge(*s_bo_ps.at(run, j + 1))
                            if j >= 2:
                                act.wait_ge(*s_merged.at(run, j - 1))
                            elif b:
                                act.wait_ge(*s_merged.at(run - 1, KT - 1 + j))
                            for v, (a, m) in enumerate(streams(l)):
                                last = fn(branch[:, j % 2, a:a + m], bank(2 * (j % 2) + v, m))
                            last.then_inc(s_bo_sb.sem, 1)
                for g in range(2 * n):
                    c, i = divmod(g, n)
                    act.wait_ge(*s_y_ps.at(l, g + 1))
                    fn(y_tm[:, i, c * COLS:(c + 1) * COLS], bank(4 + g % 4)).then_inc(s_y_sb.sem, 1)
                    if c:
                        act.wait_ge(*s_y_sb.at(l, g + 1))
                        fn(rc[:, RD:RD + DM], y_tm[:, i, :], ACT.Square,
                           accum_out=ss[:, SY + i:SY + i + 1]).then_inc(s_y_sq.sem, 1)
                        act.wait_ge(*s_y_sq.at(2 * l, i + 1))
                root(SY, n, DM, s_post_rms)
                norm_sums(2 * l + 1, rc[:, RD:RD + DM])
                norm_drain(2 * l + 1, 1)
                for f in range(2):
                    with act.Fori(0, 2) as turn:
                        for g in range(8):
                            act.wait_ge(*s_hid_ps.at(l, 16 * f + 8 * turn + g + 1))
                            for v, (a, m) in enumerate(streams(l)):
                                last = fn(hid[:, 8 * turn + g, a:a + m], bank(2 * (g % 2) + v, m), ACT.Relu)
                            last.then_inc(s_hid_relu.sem, 1)
                    if f == 0:
                        for c in range(2):
                            for i in range(n):
                                act.wait_ge(*s_ff_ps.at(l, c * (1 + n) + 2 + i))
                                fn(y_tm[:, i, c * COLS:(c + 1) * COLS], bank(i)).then_inc(s_ff_copied.sem, 1)
                junk = ht[:, 0:2, :].rearrange("p k n -> p (k n)")[:, 0:DM]
                for i in range(n):
                    act.wait_ge(*s_ff_added.at(l, n + i + 1))
                    fn(junk, y_tm[:, i, :], ACT.Square, accum_out=ss[:, SY + i:SY + i + 1]).then_inc(s_y_sq.sem, 1)
                    act.wait_ge(*s_y_sq.at(2 * l + 1, i + 1))
                root(SY, n, DM, s_post_rms)
            second_act(act, ch, fn, root, norm_sums, norm_drain)

        @block.tensor
        def _(pe):
            def take(ahead=0):
                n = take.blocks
                take.blocks += 1
                pe.wait_ge(wl[n % 2], 16 * (n // 2 + 1 + ahead))
                return n % 2

            take.blocks = 0

            def turn(out_, in_):
                k = in_.shape[0]
                return pe.transpose(out_, in_, ident[0:k, 0:k])

            def product(b, slot, j, rhs, ss_):
                for k in range(KT):
                    for v, (a, m) in enumerate(ss_):
                        last = pe.matmul(bank(b + v, m), ring[:, slot, k, j * P:(j + 1) * P], rhs[:, k, a:a + m],
                                         start=k == 0, stop=k == KT - 1)
                return last

            def channel_major(name, run, used, n, base, rhs, l, before, j0=0):
                for g in range(j0, j0 + 4 * n):
                    if g % 4 == 0:
                        slot = take()
                    if g - j0 >= 2:
                        pe.wait_ge(*used.at(run, g - 1))
                    elif g == j0:
                        for w in before:
                            pe.wait_ge(*w)
                    product(base + 2 * (g % 2), slot, g % 4, rhs, streams(l)).then_inc(name.sem, 1)

            def token_major(name, run, used, g0, n, lhs, before, width=COLS):
                slot = take()
                for w in before:
                    pe.wait_ge(*w)
                for i in range(n):
                    g = g0 + i
                    if g >= 4:
                        pe.wait_ge(*used.at(run, g - 3))
                    for k in range(KT):
                        last = pe.matmul(bank(4 + g % 4, width), lhs[:, k, i * P:(i + 1) * P], ring[:, slot, k, 0:width],
                                         start=k == 0, stop=k == KT - 1)
                    last.then_inc(name.sem, 1)

            def norm(run, rows, before):
                n = NORM_T[run]
                for w in before:
                    pe.wait_ge(*w)
                pe.wait_ge(*s_norm_xn.at(run, n))
                for j in range(KT):
                    if j >= 2:
                        pe.wait_ge(*s_norm_ht.at(run, j - 1))
                    for i in range(n):
                        last = turn(bank(2 * (j % 2) + i // 4, P, (i % 4) * P), rows[:, i, j * P:(j + 1) * P])
                    last.then_inc(s_norm_ps.sem, 1)

            def attention(l):
                us = units(l)
                heads = [u for u in range(len(us)) if us[u][4]]

                def scores(u):
                    h, col, _, tiles, _ = us[u]
                    if u >= 2:
                        pe.wait_ge(*s_att_e.at(l, u - 1))
                    q = q_cm[:, h, col:col + P]
                    key = kt[:, h // (HEADS // KVH), :]
                    if len(tiles) == AT:
                        pe.matmul(bank(2 * (u % 2)), q, key[:, 0:TOK], start=True, stop=True)
                        last = pe.matmul(bank(2 * (u % 2) + 1, CTX), q, key[:, TOK:NALL], start=True, stop=True)
                    else:
                        last = pe.matmul(bank(2 * (u % 2), CTX), q, key[:, TOK:NALL], start=True, stop=True)
                    last.then_inc(s_att_s.sem, 1)

                pe.wait_ge(*s_qk_cm.at(l, HEADS + KVH))
                pe.wait_ge(*s_gv_sb.at(l, 2 * NT[l]))
                def head(u):
                    h, col, _, tiles, _ = us[u]
                    o = heads.index(u)
                    pe.wait_ge(*s_att_pt.at(l, u + 1))
                    if o >= 2:
                        pe.wait_ge(*s_att_sb.at(l, o - 1))
                    m = TOK if col < TOK else CTX
                    v0 = KVH * HD + (h // (HEADS // KVH)) * HD
                    for k, kt_ in enumerate(tiles):
                        last = pe.matmul(bank(6 + o % 2, m), kv[:, kt_, v0:v0 + HD], PT[:, k, 0:m],
                                         start=k == 0, stop=k == len(tiles) - 1)
                    last.then_inc(s_att_o.sem, 1)

                scores(0)
                scores(1)
                for u in range(len(us)):
                    if u + 2 < len(us):
                        scores(u + 2)
                    pe.wait_ge(*s_att_p.at(l, u + 1))
                    if u:
                        pe.wait_ge(*s_att_pt.at(l, u))
                    for k in range(len(us[u][3])):
                        last = turn(bank(4, P, k * P), probs[u % 3][:, k * P:(k + 1) * P])
                    last.then_inc(s_att_t.sem, 1)
                    if u - 1 in heads:
                        head(u - 1)
                head(len(us) - 1)

            pe.wait_ge(*s_const_in.at(0, 32))
            pe.wait_ge(*s_c_silu.at(0, 1))
            for j in range(KT):
                last = turn(bank(4, 2, 2 * j), rb[0:2, j * P:(j + 1) * P])
            last.then_inc(s_c_turned.sem, 1)
            for l in range(DEPTH):
                n = NT[l]
                pe.wait_ge(*s_c_ready.at(0, 1))
                if l:
                    pe.wait_ge(*s_ff_added.at(l - 1, 2 * NT[l - 1]))
                for g in range(12):
                    slot = take()
                    if g >= 4:
                        pe.wait_ge(*s_ada_row.at(l, g - 3))
                    for k in range(KT):
                        last = pe.matmul(bank(g % 4)[0:2, :], ccol[:, k, :], ring[:, slot, k, :],
                                         start=k == 0, stop=k == KT - 1)
                    last.then_inc(s_ada_ps.sem, 1)
                pe.wait_ge(*s_ada_row.at(l, 12))
                for p, part in enumerate((0, 1, 3, 4)):
                    for j in range(KT):
                        last = turn(bank(4, 2, 2 * (KT * p + j)), ra[0:2, part * DM + j * P:part * DM + (j + 1) * P])
                last.then_inc(s_cols_ps.sem, 1)
                pe.wait_ge(*s_vecs_in.at(l, 16 * 7))
                for j in range(KT):
                    last = turn(bank(5, NVEC, NVEC * j), rc[0:NVEC, j * P:(j + 1) * P])
                last.then_inc(s_cols_ps.sem, 1)
                norm(2 * l, gv_tm, ())
                pe.wait_ge(*s_norm_ht.at(2 * l, KT))
                for b in range(2):
                    token_major(s_qkv_ps, l, s_qkv_sb, b * n, n, ht, [s_cols_ready.at(l, 1)] if b == 0 else ())
                token_major(s_qkv_ps, l, s_qkv_sb, 2 * n, AT, ht, ())
                channel_major(s_gu_ps, l, s_gu_sb, 2, 0, ht, l, ())
                for c in range(2):
                    token_major(s_gv_ps, l, s_gv_sb, c * n, n, ht, [s_qkv_sb.at(l, 2 * n + AT)] if c == 0 else ())
                pe.wait_ge(*s_qkv_roped.at(l, 1))
                pe.wait_ge(*s_gu_sb.at(l, KT))
                for h in range(HEADS + KVH):
                    if h >= 2:
                        pe.wait_ge(*s_qk_cm.at(l, h - 1))
                    for i in range(n if h < HEADS else AT):
                        src = (q_tm[:, h // 4, i, (h % 4) * HD:(h % 4 + 1) * HD] if h < HEADS
                               else kv[:, i, (h - HEADS) * HD:(h - HEADS + 1) * HD])
                        last = turn(bank(2 * (h % 2) + i // 4, P, (i % 4) * P), src)
                    last.then_inc(s_qk_ps.sem, 1)
                attention(l)
                pe.wait_ge(*s_ws_in.at(l, 32))
                pe.wait_ge(*s_att_e.at(l, UN[l]))
                for g in range(4):
                    last = turn(bank(0, P, g * P), ws_raw[:, g, :])
                last.then_inc(s_ws_ps.sem, 1)
                pe.wait_ge(*s_ws_ready.at(l, 1))
                pe.wait_ge(*s_gv_ready.at(l, 1))
                for j in range(KT):
                    if j >= 2:
                        pe.wait_ge(*s_sv_ready.at(l, j - 1))
                    for i in range(n):
                        last = pe.matmul(bank(2 * (j % 2) + i // 4, P, (i % 4) * P), gv_tm[:, i, j * P:(j + 1) * P],
                                         ws_t[:, j // 2, :], start=True, stop=True)
                    last.then_inc(s_sv_ps.sem, 1)
                channel_major(s_cgb_ps, l, s_cgb_sb, 2, 4, ht, l, [s_att_pt.at(l, UN[l]), s_att_sb.at(l, OH[l])])
                channel_major(s_cga_ps, l, s_glu_ready, 2, 0, ht, l, [s_sv_ready.at(l, KT)])
                for b, rhs in enumerate((u_cm, q_cm, u_cm)):
                    run = 3 * l + b
                    if b == 2:
                        pe.wait_ge(*s_conv_ready.at(l, KT))
                        pe.wait_ge(*s_bg_sb.at(run - 1, KT))
                        for j in range(KT):
                            for v, (a, m) in enumerate(streams(l)):
                                last = pe.matmul(bank(4 + v, m), ones[:, :], conv_slot(j, v * (TOK + 2 * PAD), m),
                                                 start=j == 0, stop=j == KT - 1)
                        last.then_inc(s_mean_ps.sem, 1)
                    for c in range(2):
                        if c:
                            before = [s_bg_sb.at(run, 4)]
                        elif b:
                            before = [s_bg_sb.at(run - 1, KT)]
                        else:
                            before = [s_cgb_sb.at(l, KT)]
                        if b == 2:
                            before = before + [s_std_sb.at(l, 1) if c else s_mean_sb.at(l, 1)]
                        channel_major(s_bg_ps, run, s_bg_sb, 1, 4, ht, l, before, j0=4 * c)
                        if b == 2 and c == 0:
                            pe.wait_ge(*s_squared.at(l, KT))
                            pe.wait_ge(*s_bg_sb.at(run, 4))
                            for j in range(KT):
                                for v, (a, m) in enumerate(streams(l)):
                                    last = pe.matmul(bank(6 + v, m), ones[:, :], u_cm[:, j, a:a + m],
                                                     start=j == 0, stop=j == KT - 1)
                            last.then_inc(s_var_ps.sem, 1)
                            pe.wait_ge(*s_conv_cm.at(l, KT))
                        if c:
                            before = [s_bo_sb.at(run, 4)]
                        elif b:
                            before = [s_bo_sb.at(run - 1, KT)]
                        else:
                            before = [s_glu_ready.at(l, KT)]
                        channel_major(s_bo_ps, run, s_bo_sb, 1, 0, rhs, l, before, j0=4 * c)
                for c in range(2):
                    token_major(s_y_ps, l, s_y_sb, c * n, n, acc,
                                [s_merged.at(3 * l + 2, KT), s_bg_sb.at(3 * l + 2, KT)] if c == 0 else ())
                norm(2 * l + 1, xn_b, [s_bo_sb.at(3 * l + 2, KT)])
                pe.wait_ge(*s_norm_ht.at(2 * l + 1, KT))
                for f in range(2):
                    if f:
                        pe.wait_ge(*s_ff_copied.at(l, 2 * n))
                    n0 = take.blocks
                    with pe.Fori(0, 2) as turn_:
                        for g in range(8):
                            if g % 4 == 0:
                                take.blocks = n0 + g // 4
                                slot = take(turn_)
                            if g >= 2:
                                pe.wait_ge(*s_hid_relu.at(l, 16 * f + 8 * turn_ + g - 1))
                            product(2 * (g % 2), slot, g % 4, ht, streams(l)).then_inc(s_hid_ps.sem, 1)
                        pe.wait_ge(*s_hid_relu.at(l, 16 * f + 8 * turn_ + 8))
                    take.blocks = n0 + 4
                    pe.wait_ge(*s_hid_ready.at(l, 16 * f + 16))
                    for c in range(2):
                        for kb in range(2):
                            slot = take()
                            for i in range(n):
                                if kb == 0:
                                    if c:
                                        pe.wait_ge(*(s_ff_copied, s_ff_added)[f].at(l, i + 1))
                                    elif i == 4:
                                        pe.wait_ge(*s_norm_ht.at(2 * l + 1, KT))
                                for k in range(KT):
                                    last = pe.matmul(bank(i), hid[:, KT * kb + k, i * P:(i + 1) * P],
                                                     ring[:, slot, k, :], start=kb == 0 and k == 0,
                                                     stop=kb == 1 and k == KT - 1)
                                if kb or i == n - 1:
                                    last.then_inc(s_ff_ps.sem, 1)
            second_pe(pe, take, turn, norm, product, token_major)

        @block.vector
        def _(dve):
            ch = Chain(dve, chain_sem["dve"])
            tt, ts, stt = dve.tensor_tensor, dve.tensor_scalar, dve.scalar_tensor_tensor

            def reciprocal(at, n):
                ch.link(dve.reciprocal(rstd[:, at:at + n], ss[:, at:at + n]))

            def norm_rows(run, rows):
                dve.wait_ge(*s_norm_rms.at(run, 1))
                reciprocal(SN, NORM_T[run])
                for i in range(NORM_T[run]):
                    ts(rows[:, i, :], x[:, i, :], rstd[:, SN + i:SN + i + 1], None, ALU.mult).then_inc(s_norm_xn.sem, 1)

            def post_rows(run, l, rows):
                dve.wait_ge(*s_post_in.at(run, 48))
                for v in range(len(streams(l))):
                    ch.link(tt(rows[:, v * DM:(v + 1) * DM], rows[:, v * DM:(v + 1) * DM], rows[:, 2 * DM:3 * DM],
                               ALU.mult))

            def post_scale(run, i, rows):
                v = i // MT
                dve.wait_ge(*s_y_sq.at(run, i + 1))
                ch.note(tt(y_tm[:, i, :], y_tm[:, i, :], rows[:, v * DM:(v + 1) * DM], ALU.mult))

            def post_add(run, l):
                n = NT[l]
                dve.wait_ge(*s_post_rms.at(run, 1))
                ch.meet()
                reciprocal(SY, n)
                for i in range(n):
                    last = stt(x[:, i, :], y_tm[:, i, :], rstd[:, SY + i:SY + i + 1], x[:, i, :],
                               op0=ALU.mult, op1=ALU.add)
                    if i < n - 1:
                        last.then_inc(s_x_added.sem, 1)
                last.then_inc(s_x_ready.sem, 1)

            def softmax(l):
                us = units(l)

                def peak(u):
                    nk = len(us[u][3])
                    dve.wait_ge(*s_att_s.at(l, u + 1))
                    ch.link(dve.tensor_reduce(red[:, 6 + u % 2:7 + u % 2], bank(2 * (u % 2), nk * P), AX.X, ALU.max))
                    ts(red[:, u % 2:u % 2 + 1], red[:, 6 + u % 2:7 + u % 2], -(HD ** -0.5), None, ALU.mult).then_inc(s_att_mx.sem, 1)

                peak(0)
                peak(1)
                for u in range(len(us)):
                    nk = len(us[u][3])
                    dve.wait_ge(*s_att_e.at(l, u + 1))
                    ch.link(dve.reciprocal(red[:, 4 + u % 2:5 + u % 2], red[:, 2 + u % 2:3 + u % 2]))
                    pr = probs[u % 3][:, 0:nk * P]
                    ts(pr, pr, red[:, 4 + u % 2:5 + u % 2], None, ALU.mult).then_inc(s_att_p.sem, 1)
                    if u + 2 < len(us):
                        peak(u + 2)

            def normalise_heads(l):
                n = NT[l]
                dve.wait_ge(*s_qkv_rms.at(l, 1))
                reciprocal(SQ, 8 * n + 2 * AT)
                dve.wait_ge(*s_gain_in.at(l, 32))
                tiles = [(b, i) for b in range(3) for i in range(n if b < 2 else AT)]
                for u, (b, i) in enumerate(tiles):
                    heads = 4 if b < 2 else KVH
                    src = q_tm[:, b, i, :] if b < 2 else kv[:, i, 0:KVH * HD]
                    at = SQ + 4 * u if b < 2 else SQ + 8 * n + 2 * i
                    for h in range(heads):
                        piece = src[:, h * HD:(h + 1) * HD]
                        ch.note(stt(piece, piece, rstd[:, at + h:at + h + 1], gains[:, b // 2, :],
                                    op0=ALU.mult, op1=ALU.mult))
                    ch.meet()
                    if i >= MT:
                        continue
                    w = heads * HD
                    xc, xs = ra[:, 4096:4096 + w], ra[:, 4608:4608 + w]

                    def halves(ap):
                        return ap.rearrange("p (h d) -> p h d", d=HD // 2)

                    for dst, at2 in ((xc, 0), (xs, HD // 2)):
                        row = rope[:, i, at2:at2 + HD // 2].unsqueeze(1).to_broadcast([P, 2 * heads, HD // 2])
                        ch.note(tt(halves(dst), halves(src), row, ALU.mult))
                    ch.meet()

                    def half(ap, s):
                        return ap.rearrange("p (h s d) -> p h s d", s=2, d=HD // 2)[:, :, s, :]

                    ch.note(tt(half(src, 0), half(xc, 0), half(xs, 1), ALU.subtract))
                    ch.link(tt(half(src, 1), half(xc, 1), half(xs, 0), ALU.add))
                ts(red[:, 8:9], eps[:, 0:1], 1.0, None, ALU.mult).then_inc(s_qkv_roped.sem, 1)

            def convolve(l):
                n = TOK if NT[l] == MT else GW - 2 * PAD
                halves = ((0, n // 2), (n // 2, n - n // 2))
                with dve.Fori(0, KT) as j:
                    ch.enter(j, 2 * CONVK - 1)
                    for a, m in halves:
                        ch.note(ts(conv_slot(j, a, m), conv_slot(j + 1, a, m), vec[:, j, 0:1],
                                   vec[:, j, CONVK + 2:CONVK + 3], ALU.mult, ALU.add))
                    for k in range(1, CONVK):
                        for a, m in halves:
                            ch.meet(back=1)
                            step = stt(conv_slot(j, a, m), conv_slot(j + 1, a + k, m), vec[:, j, k:k + 1],
                                       conv_slot(j, a, m), op0=ALU.mult, op1=ALU.add)
                            if k < CONVK - 1 or a == 0:
                                ch.note(step)
                    step.then_inc(s_conv_ready.sem, 1)
                    dve.wait_ge(*s_conv_ready.at(l, j + 1))
                    ch.leave(KT)

            def conv_norm(l):
                dve.wait_ge(*s_mean_ps.at(l, 1))
                dve.wait_ge(*s_merged.at(3 * l + 1, KT))
                for v, (a, m) in enumerate(streams(l)):
                    last = ts(kt[:, 0, a:a + m], bank(4 + v, m), 1.0 / DM, None, ALU.mult)
                last.then_inc(s_mean_sb.sem, 1)
                dve.wait_ge(*s_mean_sb.at(l, 1))
                dve.wait_ge(*s_conv_ready.at(l, KT))
                for j in range(KT):
                    for v, (a, m) in enumerate(streams(l)):
                        slot = conv_slot(j, v * (TOK + 2 * PAD), m)
                        last = tt(slot, slot, kt[:, 0, a:a + m], ALU.subtract)
                    last.then_inc(s_centred.sem, 1)
                dve.wait_ge(*s_std_sb.at(l, 1))
                ch.link(dve.reciprocal(kt[:, 1, 0:NT[l] * P], kt[:, 1, 0:NT[l] * P]))
                dve.wait_ge(*s_squared.at(l, KT))
                for j in range(KT):
                    for v, (a, m) in enumerate(streams(l)):
                        slot = conv_slot(j, v * (TOK + 2 * PAD), m)
                        last = tt(slot, slot, kt[:, 1, a:a + m], ALU.mult)
                    last.then_inc(s_normed.sem, 1)

            dve.memset(ones[:, :], 1.0)
            dve.memset(eps[:, :], EPS).then_inc(s_consts.sem, 1)
            dve.wait_ge(*s_c_turned.at(0, 1))
            dve.tensor_copy(ccol[:, :, :], bank(4, 2 * KT).rearrange("p (k v) -> p k v", v=2)).then_inc(s_c_ready.sem, 1)
            for l in range(DEPTH):
                n = NT[l]
                dve.wait_ge(*s_adab_in.at(l, 32))
                for g in range(12):
                    dve.wait_ge(*s_ada_ps.at(l, g + 1))
                    a = slice(g * COLS, (g + 1) * COLS)
                    tt(ra[0:2, a], bank(g % 4)[0:2, :], rb[0:2, a], ALU.add).then_inc(s_ada_row.sem, 1)
                dve.wait_ge(*s_cols_ps.at(l, 2))
                ch.note(dve.tensor_copy(modc[:, :, :, :], bank(4, 64).rearrange("p (a k v) -> p a k v", a=4, v=2)))
                ch.link(dve.tensor_copy(vec[:, :, :], bank(5, KT * NVEC).rearrange("p (k r) -> p k r", k=KT)))
                for part, r in ((0, CONVK), (1, CONVK + 5)):
                    last = stt(fused[:, part, :, :], modc[:, 2 * part + 1, :, :], 1.0,
                               vec[:, :, r:r + 1].to_broadcast([P, KT, 2]), op0=ALU.add, op1=ALU.mult)
                last.then_inc(s_cols_ready.sem, 1)
                norm_rows(2 * l, gv_tm)
                g = 0
                for b in range(3):
                    for i in range(n if b < 2 else AT):
                        dve.wait_ge(*s_qkv_sb.at(l, g + 1))
                        heads = 4 if b < 2 else KVH
                        at = SQ + 4 * g if b < 2 else SQ + 8 * n + 2 * i
                        sq = ra[:, 512 * (g % 8):512 * (g % 8) + heads * HD]
                        dve.tensor_reduce(ss[:, at:at + heads], sq.rearrange("p (h d) -> p h d", h=heads),
                                              AX.X, ALU.add).then_inc(s_qkv_red.sem, 1)
                        g += 1
                normalise_heads(l)
                dve.wait_ge(*s_gv_rms.at(l, 1))
                reciprocal(SG, n)
                for i in range(n):
                    last = ts(gv_tm[:, i, :], gv_tm[:, i, :], rstd[:, SG + i:SG + i + 1], None, ALU.mult)
                last.then_inc(s_gv_ready.sem, 1)
                softmax(l)
                for j in range(KT):
                    dve.wait_ge(*s_sv_ps.at(l, j + 1))
                    for v, (a, m) in enumerate(streams(l)):
                        tmp = rb[:, 1536 + 768 * (j % 2) + a:1536 + 768 * (j % 2) + a + m]
                        ch.note(stt(tmp.rearrange("p (c q) -> p c q", q=P),
                                    bank(2 * (j % 2) + v, m).rearrange("p (c q) -> p c q", q=P),
                                    vec[:, j, CONVK + 1:CONVK + 2],
                                    bs_row[:, j // 2, :].unsqueeze(1).to_broadcast([P, m // P, P]),
                                    op0=ALU.mult, op1=ALU.add))
                    ch.meet()
                    tmp = rb[:, 1536 + 768 * (j % 2):1536 + 768 * (j % 2) + n * P]
                    tt(u_cm[:, j, 0:n * P], u_cm[:, j, 0:n * P], tmp, ALU.mult).then_inc(s_sv_ready.sem, 1)
                for j in range(KT):
                    dve.wait_ge(*s_cga_ps.at(l, j + 1))
                    dve.wait_ge(*s_cgb_sb.at(l, j + 1))
                    for v, (a, m) in enumerate(streams(l)):
                        slot = conv_slot(j + 1, PAD + v * (TOK + 2 * PAD), m)
                        last = tt(slot, slot, bank(2 * (j % 2) + v, m), ALU.mult)
                    last.then_inc(s_glu_ready.sem, 1)
                dve.wait_ge(*s_glu_ready.at(l, KT))
                convolve(l)
                conv_norm(l)
                post_rows(2 * l, l, rc)
                for i in range(n):
                    post_scale(2 * l, i, rc)
                post_add(2 * l, l)
                dve.wait_ge(*s_x_ready.at(2 * l, 1))
                norm_rows(2 * l + 1, xn_b)
                for f in range(2):
                    with dve.Fori(0, 2) as turn:
                        for g in range(8):
                            dve.wait_ge(*s_hid_relu.at(l, 16 * f + 8 * turn + g + 1))
                            h = hid[:, 8 * turn + g, 0:n * P]
                            tt(h, h, h, ALU.mult).then_inc(s_hid_ready.sem, 1)
                    if f:
                        post_rows(2 * l + 1, l, rb)
                        for c in range(2):
                            for i in range(n):
                                dve.wait_ge(*s_ff_ps.at(l, (2 + c) * (1 + n) + 2 + i))
                                piece = y_tm[:, i, c * COLS:(c + 1) * COLS]
                                tt(piece, piece, bank(i), ALU.add).then_inc(s_ff_added.sem, 1)
                                if c and i:
                                    post_scale(2 * l + 1, i - 1, rb)
                post_scale(2 * l + 1, n - 1, rb)
                post_add(2 * l + 1, l)
                dve.wait_ge(*s_x_ready.at(2 * l + 1, 1))
            second_dve(dve, ch, norm_rows)


def shape_constants():
    tok = np.arange(TOK)
    inv = (np.float32(10000.0) ** (-np.arange(HD // 4, dtype=np.float32) / np.float32(HD // 4))).astype(np.float32)
    ang = np.concatenate([(tok // 64)[:, None].astype(np.float32) * inv,
                          (tok % 64)[:, None].astype(np.float32) * inv], axis=-1)
    i, j = np.arange(P)[:, None], np.arange(P)[None, :]
    same = i // 64 == j // 64
    big = 1e30
    masks = [same & (i <= j),
             np.where(same & (j < i), 0.0, big),
             np.where(same & (i <= j), 0.0, -big),
             (i // 2 == j // 2) & (j < i), (i // 2 == j // 2) & (i < j)]
    for s in (2, 4, 8, 16, 32):
        masks.append((i // (2 * s) == j // (2 * s)) & (i // s < j // s))
    masks += [same, (i < 64) & (j >= 0), (i >= 64) & (j >= 0)]
    bands = []
    for w in (2, 4, 8, 16):
        inside = (i <= j) & (i > j - w)
        bands += [inside / np.minimum(j + 1, w) - (i == j), inside / w - (i == j), (i - P > j - w) / w]
    ends = np.arange(32) * 16 + 31
    ok = (ends[None, :] <= tok[:, None]) & (np.arange(32) < 31)[None, :]
    return {
        "ident": np.eye(P, dtype=np.float32),
        "rope": np.concatenate([np.cos(ang), np.sin(ang)], axis=-1).astype(np.float32),
        "masks": np.stack([np.asarray(m, np.float32) for m in masks]),
        "bands": np.stack([np.asarray(m, np.float32) for m in bands]),
        "causal": np.where(j <= i, 0.0, -big).astype(np.float32),
        "cneg": np.where(ok, 0.0, -big).astype(np.float32),
        "cmask": ok.astype(np.float32),
    }


def kernel(**inputs):
    import concourse.bacc as bacc
    from concourse.bass_utils import run_bass_kernel_spmd

    nc = bacc.Bacc("TRN2", target_bir_lowering=False, num_devices=1)
    arrays, drams = {}, {}
    for name, value in {**inputs, **shape_constants()}.items():
        a = np.ascontiguousarray(value)
        arrays[f"in_{name}"] = a
        drams[name] = nc.dram_tensor(f"in_{name}", a.shape, mybir.dt.from_np(a.dtype), kind="ExternalInput").ap()
    out = nc.dram_tensor("out_x", (1, TOK, DM), F32, kind="ExternalOutput").ap()
    build_program(nc, drams, out[0].rearrange("(t p) d -> p t d", p=P))
    r = run_bass_kernel_spmd(nc, [arrays], core_ids=[0])
    return r.results[0]["out_x"]
```
